# Optimizing a Trainium2 kernel written in Bass

```python
import jax, jax.numpy as jnp
from jax import lax
import numpy as np

D_MODEL = 1024
BATCH = 1
SEQ = 512
DEPTH = 1

PLE_DIM = 256
ATTN_HEADS = 8
ATTN_HEAD_DIM = 64
ATTN_WIDTH = ATTN_HEADS * ATTN_HEAD_DIM
Q_BLOCK = 128
CONV_WIDTH = ATTN_WIDTH
CONV_K = 3
N_BRANCH = 2
PEER_HEADS = 8
PEER_NKEYS = 128
PEER_N_EXPERTS = PEER_NKEYS * PEER_NKEYS
PEER_QDIM = 256
PEER_HALF = PEER_QDIM // 2
PEER_TOPK = 16
TOKEN_CHUNK = 128
EPS = 1e-6

IN_SIZES = [ATTN_WIDTH, ATTN_WIDTH, ATTN_WIDTH, ATTN_HEADS,
            CONV_WIDTH, CONV_WIDTH, CONV_WIDTH, D_MODEL, D_MODEL]
IN_TOTAL = sum(IN_SIZES)
IN_SPLITS = np.cumsum(IN_SIZES)[:-1].tolist()

kernel_name = "fox_shortconv_peer_hybrid"

def rmsnorm(x, g):
    xf = x.astype(jnp.float32)
    y = xf * lax.rsqrt(jnp.mean(xf * xf, axis=-1, keepdims=True) + EPS) * g.astype(jnp.float32)
    return y.astype(x.dtype)

def forgetting_attention(q, k, v, f_logit):
    B, S, H, Dh = q.shape
    nb = S // Q_BLOCK
    log_f = jax.nn.log_sigmoid(f_logit.astype(jnp.float32))
    c = jnp.cumsum(log_f, axis=1).transpose(0, 2, 1)
    qb = q.reshape(B, nb, Q_BLOCK, H, Dh).transpose(1, 0, 3, 2, 4)
    cqb = c.reshape(B, H, nb, Q_BLOCK).transpose(2, 0, 1, 3)
    kt = k.transpose(0, 2, 1, 3)
    vt = v.transpose(0, 2, 1, 3)
    k_pos = jnp.arange(S)
    scale = ATTN_HEAD_DIM ** -0.5

    def block(args):
        qi, cqi, i = args
        logits = (jnp.einsum('bhqd,bhkd->bhqk', qi, kt).astype(jnp.float32) * scale
                  + cqi[..., :, None] - c[:, :, None, :])
        q_pos = i * Q_BLOCK + jnp.arange(Q_BLOCK)
        mask = k_pos[None, :] <= q_pos[:, None]
        logits = jnp.where(mask, logits, -jnp.inf)
        w = jax.nn.softmax(logits, axis=-1)
        return jnp.einsum('bhqk,bhkd->bhqd', w.astype(vt.dtype), vt)

    out = lax.map(block, (qb, cqb, jnp.arange(nb)))
    return out.transpose(1, 0, 3, 2, 4).reshape(B, S, H * Dh)

def causal_depthwise_conv(z, w):
    C = z.shape[-1]
    return lax.conv_general_dilated(
        z, w[:, None, :].astype(z.dtype), window_strides=(1,),
        padding=[(CONV_K - 1, 0)], dimension_numbers=('NWC', 'WIO', 'NWC'),
        feature_group_count=C)

def peer(h, w_q, k1, k2, u, v):
    B, S, D = h.shape
    q = jnp.einsum('bsd,dhe->bshe', h, w_q)
    s1 = jnp.einsum('bshe,hne->bshn', q[..., :PEER_HALF], k1).astype(jnp.float32)
    s2 = jnp.einsum('bshe,hne->bshn', q[..., PEER_HALF:], k2).astype(jnp.float32)
    v1, i1 = lax.top_k(s1, PEER_TOPK)
    v2, i2 = lax.top_k(s2, PEER_TOPK)
    cand_s = (v1[..., :, None] + v2[..., None, :]).reshape(B, S, PEER_HEADS, PEER_TOPK * PEER_TOPK)
    cand_i = (i1[..., :, None] * PEER_NKEYS + i2[..., None, :]).reshape(B, S, PEER_HEADS, PEER_TOPK * PEER_TOPK)
    top_s, top_j = lax.top_k(cand_s, PEER_TOPK)
    ids = jnp.take_along_axis(cand_i, top_j, axis=-1)
    gates = jax.nn.softmax(top_s, axis=-1)
    T = B * S
    nc = T // TOKEN_CHUNK
    hf = h.reshape(nc, TOKEN_CHUNK, D)
    idf = ids.reshape(nc, TOKEN_CHUNK, PEER_HEADS, PEER_TOPK)
    gf = gates.reshape(nc, TOKEN_CHUNK, PEER_HEADS, PEER_TOPK)

    def chunk(args):
        hc, ic, gc = args
        u_sel = u[ic]
        act = jax.nn.gelu(jnp.einsum('td,thkd->thk', hc, u_sel), approximate=False)
        wgt = gc.astype(hc.dtype) * act
        return jnp.einsum('thk,thkd->td', wgt, v[ic])

    return lax.map(chunk, (hf, idf, gf)).reshape(B, S, D)

def setup_inputs(seed: int = 0) -> dict:
    key = jax.random.key(seed)
    ks = jax.random.split(key, 20)
    D = D_MODEL
    f32 = jnp.float32
    nrm = lambda k, shape, s: jax.random.normal(k, shape, f32) * s
    return {
        "x": nrm(ks[0], (BATCH, SEQ, D), 1.0),
        "p": nrm(ks[1], (DEPTH, BATCH, SEQ, PLE_DIM), 1.0),
        "g_mix": 1.0 + nrm(ks[2], (DEPTH, D), 0.02),
        "w_in": nrm(ks[3], (DEPTH, D, IN_TOTAL), D ** -0.5),
        "b_f": jax.random.uniform(ks[4], (DEPTH, ATTN_HEADS), f32, 1.0, 6.0),
        "conv_w": nrm(ks[5], (DEPTH, CONV_K, CONV_WIDTH), CONV_K ** -0.5),
        "w_branch": nrm(ks[6], (DEPTH, N_BRANCH, ATTN_WIDTH, D), ATTN_WIDTH ** -0.5),
        "w_out": nrm(ks[7], (DEPTH, D, D), D ** -0.5),
        "g_ffn": 1.0 + nrm(ks[8], (DEPTH, D), 0.02),
        "w_peer_q": nrm(ks[9], (DEPTH, D, PEER_HEADS, PEER_QDIM), D ** -0.5),
        "peer_k1": nrm(ks[10], (DEPTH, PEER_HEADS, PEER_NKEYS, PEER_HALF), PEER_HALF ** -0.5),
        "peer_k2": nrm(ks[11], (DEPTH, PEER_HEADS, PEER_NKEYS, PEER_HALF), PEER_HALF ** -0.5),
        "peer_u": nrm(ks[12], (DEPTH, PEER_N_EXPERTS, D), D ** -0.5),
        "peer_v": nrm(ks[13], (DEPTH, PEER_N_EXPERTS, D), PEER_HEADS ** -0.5),
        "g_ple": 1.0 + nrm(ks[14], (DEPTH, D), 0.02),
        "w_ple_gate": nrm(ks[15], (DEPTH, D, D), D ** -0.5),
        "w_ple_proj": nrm(ks[16], (DEPTH, PLE_DIM, D), PLE_DIM ** -0.5),
        "g_final": 1.0 + nrm(ks[17], (D,), 0.02),
    }

def reference(x, p, g_mix, w_in, b_f, conv_w, w_branch, w_out, g_ffn, w_peer_q,
              peer_k1, peer_k2, peer_u, peer_v, g_ple, w_ple_gate, w_ple_proj, g_final):
    B, S, D = x.shape
    for i in range(DEPTH):
        h = rmsnorm(x, g_mix[i])
        proj = h @ w_in[i]
        q, k, v, f_logit, gb, gc_in, xc, g_attn, g_conv = jnp.split(proj, IN_SPLITS, axis=-1)
        attn = forgetting_attention(
            q.reshape(B, S, ATTN_HEADS, ATTN_HEAD_DIM),
            k.reshape(B, S, ATTN_HEADS, ATTN_HEAD_DIM),
            v.reshape(B, S, ATTN_HEADS, ATTN_HEAD_DIM),
            f_logit + b_f[i])
        conv = gb * causal_depthwise_conv(gc_in * xc, conv_w[i])
        branches = jnp.stack([attn, conv], axis=0)
        y_br = jnp.einsum('nbsc,ncd->nbsd', branches, w_branch[i])
        gates = jax.nn.sigmoid(jnp.stack([g_attn, g_conv], axis=0))
        merged = jnp.sum(gates * y_br, axis=0)
        x = x + merged @ w_out[i]
        x = x + peer(rmsnorm(x, g_ffn[i]), w_peer_q[i], peer_k1[i], peer_k2[i], peer_u[i], peer_v[i])
        ple_gate = jax.nn.sigmoid(rmsnorm(x, g_ple[i]) @ w_ple_gate[i])
        x = x + ple_gate * (p[i] @ w_ple_proj[i])
    return rmsnorm(x, g_final)


_drawn_inputs = setup_inputs


def setup_inputs(seed=0):
    import zlib

    import numpy as np

    out = dict(_drawn_inputs(seed))
    spreads = {}
    factors = {'g_ple': 42.925, 'g_final': 8.249}
    for name, (base, spread) in spreads.items():
        noise = np.random.default_rng([zlib.crc32(name.encode()), seed]).standard_normal(out[name].shape)
        drawn = base * np.exp(spread * noise) if base else spread * noise
        out[name] = __import__('jax').numpy.asarray(drawn.astype(out[name].dtype))
    for name, factor in factors.items():
        out[name] = (out[name] * factor).astype(out[name].dtype)
    return out
```

```python
from contextlib import ExitStack

import concourse.bass as bass
from concourse import mybir

F32 = mybir.dt.float32
F32R = mybir.dt.float32r
BF16 = mybir.dt.bfloat16
U32 = mybir.dt.uint32
ALU = mybir.AluOpType
ACT = mybir.ActivationFunctionType
AX = mybir.AxisListType

P = 128
T = 512
TT = T // P
D = 1024
DC = D // P
HEADS = 8
PAIRS = HEADS // 2
HD = 64
CW = 512
CC = CW // P
TAPS = 3
PH = 8
NK = 128
TOPK = 16
HK = PH * TOPK
CAND = TOPK * TOPK
PLE = 256
EPS = 1e-6
NORM_BANK = (7, 7, 1, 7)
MASKED = -3.0e38

UW = 1024
U_V = 0
U_MIX = U_V + 4
N_MIX = 5 * PAIRS
U_MERGE = U_MIX + N_MIX
N_MERGE = 3 * DC
U_OUT = U_MERGE + N_MERGE
U_PQ = U_OUT + DC
N_PQ = 2 * PH
U_DENSE = U_PQ + N_PQ
GB = 4
GROUPS = NK // GB
U_PLE = U_DENSE + 2 * NK
N_UNITS = U_PLE + DC + 2
RAW = 4
SL = 8

MIX = ["q", "k"]
for _i in range(PAIRS):
    MIX += ["C", "x", "B"] + (["q", "k"] if _i < PAIRS - 1 else [])

GT = 64
GSUB = 16


def peer_block_kernel(nc, xT, pT, stream, w_f, b_f, conv_w, gains, keysT, gate_dram, outT):
    ctx = ExitStack()
    with ctx:
        def sb(name, shape, dt, where=ctx):
            return where.enter_context(nc.sbuf_tensor(name, shape, dt))

        def sem(name):
            return ctx.enter_context(nc.semaphore(name))

        x = sb("x", [P, DC, T], F32)
        hh = sb("hh", [P, DC, T], F32R)
        hl = sb("hl", [P, DC, T], F32R)
        raw = sb("raw", [P, RAW, UW], F32)
        wh = sb("wh", [P, SL, UW], F32R)
        wl = sb("wl", [P, SL, UW], F32R)
        ones = sb("ones", [P, P], F32)
        ident = sb("ident", [P, P], F32)
        iota_nk = sb("iota_nk", [P, NK], BF16)
        iota_k = sb("iota_k", [P, TOPK], BF16)
        gain = sb("gain", [P, 4, DC], F32)
        tick = sb("tick", [P, 1], F32)
        rstd = sb("rstd", [P, T], F32)

        mix = ExitStack()
        sq = sb("sq", [P, 2, T], F32, mix)
        hf = sb("hf", [P, 2, T], F32, mix)
        attn_h = sb("attn_h", [P, CC, T], F32R, mix)
        attn_l = sb("attn_l", [P, CC, T], F32R, mix)
        conv_h = sb("conv_h", [P, CC, T], F32R, mix)
        conv_l = sb("conv_l", [P, CC, T], F32R, mix)
        att = ExitStack()
        v_sb = sb("v_sb", [P, TT, CW], F32, att)
        qa = sb("qa", [P, 2, 2, T], F32, att)
        ka = sb("ka", [P, 2, 2, T], F32, att)
        probs = sq
        probsT = sb("probsT", [P, T], F32, att)
        c_in = hf[:, 1, :]
        cv = hf[:, 0, :]
        z = sb("z", [P, T + TAPS - 1], F32, att)
        tri = sb("tri", [P, T], F32, att)
        mask = sb("mask", [P, P], F32, att)
        wf = sb("wf", [P, DC, HEADS], F32, att)
        wf_h = sb("wf_h", [P, DC, HEADS], F32R, att)
        wf_l = sb("wf_l", [P, DC, HEADS], F32R, att)
        bfb = sb("bfb", [P, HEADS], F32, att)
        fz = sb("fz", [P, TT, HEADS], F32, att)
        fa = sb("fa", [P, TT, HEADS], F32, att)
        fe = sb("fe", [P, TT, HEADS], F32, att)
        logf = sb("logf", [P, TT, HEADS], F32, att)
        cum = sb("cum", [HEADS, T], F32, att)
        ncum = sb("ncum", [HEADS, T], F32, att)
        convw = sb("convw", [P, TAPS, CC], F32, att)
        nmax = sb("nmax", [P, 2], F32, att)
        rsum = sb("rsum", [P, 2], F32, att)
        att.close()
        mrg = ExitStack()
        merged = sb("merged", [P, DC, T], F32, mrg)
        sig_a = sb("sig_a", [P, 2, T], F32, mrg)
        sig_c = sb("sig_c", [P, 2, T], F32, mrg)
        mrg.close()
        mix.close()
        rt = ExitStack()
        sq1 = sb("sq1", [P, 2, T], F32, rt)
        hf1 = sb("hf1", [P, 2, T], F32, rt)
        i1T = sb("i1T", [P, T], F32, rt)
        i2T = sb("i2T", [P, T], F32, rt)
        g1 = sb("g1", [P, T], F32, rt)
        g2 = sb("g2", [P, T], F32, rt)
        g3 = sb("g3", [P, T], F32, rt)
        rs = ExitStack()
        keys = sb("keys", [P, N_PQ, NK], F32, rs)
        qT = hf1
        scores = sb("scores", [P, TT, N_PQ, NK], F32, rs)
        cand = sb("cand", [P, PH, TOPK, TOPK], F32, rs)
        v12 = sb("v12", [P, N_PQ, TOPK], F32, rs)
        i12 = sb("i12", [P, N_PQ, TOPK], U32, rs)
        i12b = sb("i12b", [P, N_PQ, TOPK], BF16, rs)
        top = sb("top", [P, PH, TOPK], F32, rs)
        topj = sb("topj", [P, PH, TOPK], U32, rs)
        rank = sb("rank", [P, 2, HK], U32, rs)
        rankb = sb("rankb", [P, 2, HK], BF16, rs)
        gsum = sb("gsum", [P, 2, PH], F32, rs)
        chosen = sb("chosen", [P, 3, HK], F32, rs)
        gT = sq1[:, 0, :]
        gb = sb("gb", [P, T], BF16, rs)
        rs.close()
        gs = ExitStack()
        hot = sb("hot", [P, 4, 4, NK], BF16, gs)
        stage = sb("stage", [P, NK, GT], F32, gs)
        gs.close()
        rt.close()
        ex = ExitStack()
        gate = sb("gate", [P, 2, GB, T], F32, ex)
        wt = sb("wt", [P, 2, T], F32, ex)
        act_h = sb("act_h", [P, 2, GB, T], F32R, ex)
        act_l = sb("act_l", [P, 2, GB, T], F32R, ex)
        ex.close()
        pl = ExitStack()
        sq2 = sb("sq2", [P, 2, T], F32, pl)
        hf2 = sb("hf2", [P, 2, T], F32, pl)
        pt = sb("pt", [P, 2, T], F32, pl)
        pt_h = sb("pt_h", [P, 2, T], F32R, pl)
        pt_l = sb("pt_l", [P, 2, T], F32R, pl)
        sg = sb("sg", [P, 2, T], F32, pl)
        upd = sb("upd", [P, 2, T], F32, pl)
        outb = sb("outb", [P, DC, T], F32, pl)
        pl.close()
        oh = scores[:, :, :, :].rearrange("p t u n -> p (t u n)").bitcast(BF16)

        psum = [ctx.enter_context(nc.psum_tensor(f"bank{b}", [P, T], F32)) for b in range(8)]

        x_in = [sem(f"x_in{i}") for i in range(2)]
        const_in = sem("const_in")
        keys_in = sem("keys_in")
        p_in = sem("p_in")
        raw_in = [sem(f"raw_in{i}") for i in range(RAW)]
        hi_done = sem("hi_done")
        lo_done = sem("lo_done")
        unit_used = sem("unit_used")
        consts = sem("consts")
        consts2 = sem("consts2")
        sq_ready = sem("sq_ready")
        sq_used = sem("sq_used")
        var_ready = sem("var_ready")
        std_ready = sem("std_ready")
        hf_ready = sem("hf_ready")
        hh_ready = sem("hh_ready")
        h_ready = sem("h_ready")
        v_out = sem("v_out")
        f_ready = sem("f_ready")
        f_abs = sem("f_abs")
        f_exp = sem("f_exp")
        f_ln = sem("f_ln")
        logf_ready = sem("logf_ready")
        cum_ready = sem("cum_ready")
        cum_out = sem("cum_out")
        aug_in = [sem(f"aug_in{i}") for i in range(2)]
        mix_act = sem("mix_act")
        mix_dve = sem("mix_dve")
        logits_ready = sem("logits_ready")
        max_ready = sem("max_ready")
        exp_done = sem("exp_done")
        probs_ready = sem("probs_ready")
        pT_ready = sem("pT_ready")
        pT_out = sem("pT_out")
        pv_done = sem("pv_done")
        pair_out = sem("pair_out")
        sig_done = sem("sig_done")
        mg_out = sem("mg_out")
        mh_ready = sem("mh_ready")
        ml_ready = sem("ml_ready")
        wo_out = sem("wo_out")
        pq_out = sem("pq_out")
        sc_ready = sem("sc_ready")
        sc_out = sem("sc_out")
        top_ready = sem("top_ready")
        gexp = sem("gexp")
        chosen_ready = sem("chosen_ready")
        chT_ready = sem("chT_ready")
        chT_out = sem("chT_out")
        hot_ready = sem("hot_ready")
        hot_used = sem("hot_used")
        set_out = sem("set_out")
        gate_stored = sem("gate_stored")
        gate_in = [sem(f"gate_in{i}") for i in range(2)]
        gelu_done = sem("gelu_done")
        wcopy = sem("wcopy")
        rows_ready = sem("rows_ready")
        parts_ready = sem("parts_ready")
        w_done = sem("w_done")
        wsplit = sem("wsplit")
        o_ready = sem("o_ready")
        o_out = sem("o_out")
        pp_split = sem("pp_split")
        ple_sig = sem("ple_sig")
        ple_out = sem("ple_out")
        out_ready = sem("out_ready")
        stored = sem("stored")
        dve_own = sem("dve_own")

        block = ctx.enter_context(nc.Block())

        def by_act(m):
            return sum(k in "qkC" for k in MIX[:m])

        def by_dve(m):
            return sum(k in "xB" for k in MIX[:m])

        def wait_mix_out(eng, m):
            if MIX[m] in "qkC":
                eng.wait_ge(mix_act, by_act(m) + 1)
            else:
                eng.wait_ge(mix_dve, by_dve(m) + 1)

        @block.sync
        def _(sp):
            for n in range(SL):
                if n >= RAW:
                    sp.wait_ge(lo_done, n - RAW + 1)
                sp.dma_start(raw[:, n % RAW, :], stream[n]).then_inc(raw_in[n % RAW], 16)
            with sp.Fori(1, N_UNITS // SL) as i:
                for u in range(SL):
                    sp.wait_ge(lo_done, SL * i + (u - RAW + 1))
                    sp.dma_start(raw[:, u % RAW, :],
                                 stream[bass.ds(SL * i + u, 1)].rearrange("o p w -> p (o w)")).then_inc(raw_in[u % RAW], 16)
            for n in range(N_UNITS // SL * SL, N_UNITS):
                sp.wait_ge(lo_done, n - RAW + 1)
                sp.dma_start(raw[:, n % RAW, :], stream[n]).then_inc(raw_in[n % RAW], 16)

            for c in range(DC):
                sp.wait_ge(out_ready, c + 1)
                sp.dma_start(outT[c], outb[:, c, :]).then_inc(stored, 16)
            sp.wait_ge(stored, 16 * DC)

        @block.gpsimd
        def _(pool):
            nc.gpsimd.memset(ones[:], 1.0).then_inc(consts, 1)
            nc.gpsimd.memset(ident[:], 0.0).then_inc(consts, 1)
            nc.gpsimd.memset(tri[:], 1.0).then_inc(consts, 1)
            nc.gpsimd.memset(mask[:], 0.0).then_inc(consts, 1)
            pool.wait_ge(consts, 4)
            nc.gpsimd.affine_select(out=ident[:], in_=ident[:], compare_op=ALU.not_equal, fill=1.0, base=0,
                                    pattern=[[-1, P]], channel_multiplier=1).then_inc(consts2, 1)
            nc.gpsimd.affine_select(out=tri[:], in_=tri[:], compare_op=ALU.is_ge, fill=0.0, base=0,
                                    pattern=[[1, T]], channel_multiplier=-1).then_inc(consts2, 1)
            nc.gpsimd.affine_select(out=mask[:], in_=mask[:], compare_op=ALU.is_ge, fill=MASKED, base=0,
                                    pattern=[[-1, P]], channel_multiplier=1).then_inc(consts2, 1)
            nc.gpsimd.iota(iota_nk[:], pattern=[[1, NK]], base=0, channel_multiplier=0,
                           allow_small_or_imprecise_dtypes=True).then_inc(consts2, 1)
            nc.gpsimd.iota(iota_k[:], pattern=[[1, TOPK]], base=0, channel_multiplier=0,
                           allow_small_or_imprecise_dtypes=True).then_inc(consts2, 1)

            def split(u, unit, turn, free):
                pool.wait_ge(raw_in[u % RAW], turn)
                if free is not None:
                    pool.wait_ge(unit_used, free)
                nc.gpsimd.tensor_tensor(tick[:], ones[:, 0:1], ones[:, 0:1], ALU.add)
                nc.gpsimd.tensor_copy(wh[:, u, :], raw[:, u % RAW, :]).then_inc(hi_done, 1)
                pool.wait_ge(hi_done, unit + 1)
                nc.gpsimd.tensor_tensor(wl[:, u, :], raw[:, u % RAW, :], wh[:, u, :].bitcast(F32),
                                        ALU.subtract).then_inc(lo_done, 1)

            for u in range(SL):
                split(u, u, 16 * (u // RAW + 1), None)
            with pool.Fori(1, N_UNITS // SL) as i:
                for u in range(SL):
                    split(u, SL * i + u, 32 * i + 16 * (u // RAW + 1), SL * i + (u - SL + 1))
            for n in range(N_UNITS // SL * SL, N_UNITS):
                split(n % SL, n, 16 * (n // RAW + 1), n - SL + 1)

        @block.tensor
        def _(pe):
            def three(out, ah, al, bh, bl, start, stop):
                nc.tensor.matmul(out, ah, bh, start=start, stop=False)
                nc.tensor.matmul(out, ah, bl, start=False, stop=False)
                return nc.tensor.matmul(out, al, bh, start=False, stop=stop)

            def w(part, n, c):
                return part[:, n % SL, c * P:(c + 1) * P]

            def project(n, bank, c0=0, c1=DC, h_from=None):
                for c in range(c0, c1):
                    if c == 0:
                        pe.wait_ge(lo_done, n + 1)
                    if h_from is not None:
                        pe.wait_ge(h_ready, h_from + c + 1)
                    last = three(psum[bank][:], w(wh, n, c), w(wl, n, c), hh[:, c, :], hl[:, c, :], c == 0, c == DC - 1)
                if c1 == DC:
                    last.then_inc(unit_used, 1)
                return last

            def norm_sums(k, sqb):
                for c in range(DC):
                    pe.wait_ge(sq_ready, DC * k + c + 1)
                    nc.tensor.matmul(psum[NORM_BANK[k]][:], ones[:], sqb[:, c % 2, :], start=c == 0, stop=c == DC - 1).then_inc(sq_used, 1)

            pe.wait_ge(consts2, 5)
            norm_sums(0, sq)
            for j in range(4):
                pe.wait_ge(lo_done, U_V + j + 1)
                for c in (2 * j, 2 * j + 1):
                    pe.wait_ge(h_ready, c + 1)
                    for tt in range(TT):
                        cols = slice(tt * P, (tt + 1) * P)
                        wc = slice((c % 2) * CW, (c % 2 + 1) * CW)
                        last = three(psum[tt][:], hh[:, c, cols], hl[:, c, cols], wh[:, U_V + j, wc], wl[:, U_V + j, wc],
                                     c == 0, c == DC - 1)
                last.then_inc(unit_used, 1)
            for tt in range(TT):
                cols = slice(tt * P, (tt + 1) * P)
                for c in range(DC):
                    last = three(psum[4][:, tt * HEADS:(tt + 1) * HEADS], hh[:, c, cols], hl[:, c, cols],
                                 wf_h[:, c, :], wf_l[:, c, :], c == 0, c == DC - 1)
            last.then_inc(f_ready, 1)

            pe.wait_ge(v_out, 1)
            project(U_MIX, 0)
            project(U_MIX + 1, 1)
            pe.wait_ge(logf_ready, 1)
            for j in range(TT):
                last = nc.tensor.matmul(psum[5][0:HEADS, j * P:T], logf[:, j, :], tri[:, 0:T - j * P],
                                        start=j == 0, stop=j == TT - 1)
            last.then_inc(cum_ready, 1)

            def rows(e):
                return slice(0, HD + 2) if e == 0 else slice(0, P)

            def transposes(g):
                e, qi = (g // TT) % 2, g % TT
                pe.wait_ge(probs_ready, g + 1)
                if g >= 1:
                    pe.wait_ge(pT_out, g)
                for kj in range(qi + 1):
                    last = nc.tensor.transpose(psum[5][:, kj * P:(kj + 1) * P], probs[:, g % 2, kj * P:(kj + 1) * P], ident[:])
                last.then_inc(pT_ready, 1)

            def values(g):
                pair, e, qi = g // (2 * TT), (g // TT) % 2, g % TT
                pe.wait_ge(pT_out, g + 1)
                if g % (2 * TT) == 0 and pair >= 2:
                    pe.wait_ge(pair_out, pair - 1)
                head = 2 * pair + e
                for kj in range(qi + 1):
                    last = nc.tensor.matmul(psum[6 + pair % 2][HD * e:HD * (e + 1), qi * P:(qi + 1) * P],
                                            v_sb[:, kj, head * HD:(head + 1) * HD], probsT[:, kj * P:(kj + 1) * P],
                                            start=kj == 0, stop=kj == qi)
                last.then_inc(pv_done, 1)

            m = 2
            for pair in range(PAIRS):
                units = 5 if pair < PAIRS - 1 else 3
                steps = units * DC
                for s in range(2 * TT):
                    for k in range(steps * s // (2 * TT), steps * (s + 1) // (2 * TT)):
                        mu, c = m + k // DC, k % DC
                        if c == 0 and mu >= 3:
                            wait_mix_out(pe, mu - 3)
                        last = project(U_MIX + mu, mu % 3, c, c + 1)
                    g = 2 * TT * pair + s
                    e, qi = s // TT, s % TT
                    if s == 0:
                        pe.wait_ge(aug_in[pair % 2], 64 * (pair // 2 + 1))
                        wait_mix_out(pe, 1 + 5 * pair)
                    if g >= 2:
                        pe.wait_ge(exp_done, g - 1)
                    nc.tensor.matmul(psum[3 + g % 2][:, 0:(qi + 1) * P], qa[rows(e), pair % 2, e, qi * P:(qi + 1) * P],
                                     ka[rows(e), pair % 2, e, 0:(qi + 1) * P], start=True, stop=True).then_inc(logits_ready, 1)
                    if g >= 1:
                        transposes(g - 1)
                    if g >= 2:
                        values(g - 2)
                m += units
            last_g = 2 * TT * PAIRS - 1
            transposes(last_g)
            values(last_g - 1)
            values(last_g)

            for dc in range(DC):
                n, b = U_MERGE + 3 * dc, 4 * (dc % 2)
                if dc >= 2:
                    pe.wait_ge(mg_out, dc - 1)
                elif dc == 0:
                    wait_mix_out(pe, len(MIX) - 1)
                    wait_mix_out(pe, len(MIX) - 2)
                    wait_mix_out(pe, len(MIX) - 3)
                project(n, b)
                project(n + 1, b + 1)
                pe.wait_ge(lo_done, n + 3)
                if dc == 0:
                    pe.wait_ge(pair_out, PAIRS)
                    pe.wait_ge(exp_done, 2 * TT * PAIRS)
                for br, (bh, bl) in enumerate(((attn_h, attn_l), (conv_h, conv_l))):
                    for c in range(CC):
                        last = three(psum[b + 2 + br][:], w(wh, n + 2, br * CC + c), w(wl, n + 2, br * CC + c),
                                     bh[:, c, :], bl[:, c, :], c == 0, c == CC - 1)
                last.then_inc(unit_used, 1)

            for dc in range(DC):
                if dc >= 4:
                    pe.wait_ge(wo_out, dc - 3)
                elif dc == 0:
                    pe.wait_ge(mg_out, DC)
                for c in range(DC):
                    if c == 0:
                        pe.wait_ge(lo_done, U_OUT + dc + 1)
                    if dc == 0:
                        pe.wait_ge(ml_ready, c + 1)
                    n = U_OUT + dc
                    last = three(psum[dc % 4][:], w(wh, n, c), w(wl, n, c), hh[:, c, :], hl[:, c, :], c == 0, c == DC - 1)
                last.then_inc(unit_used, 1)

            norm_sums(1, sq1)
            pe.wait_ge(keys_in, 16)

            def score(n):
                pe.wait_ge(pq_out, n + 1)
                if n >= 2:
                    pe.wait_ge(sc_out, n - 1)
                for tt in range(TT):
                    last = nc.tensor.matmul(psum[2 + n % 2][:, tt * NK:(tt + 1) * NK], qT[:, n % 2, tt * P:(tt + 1) * P],
                                            keys[:, n, :], start=True, stop=True)
                last.then_inc(sc_ready, 1)

            for n in range(N_PQ):
                if n == 0:
                    pe.wait_ge(wo_out, DC)
                if n >= 2:
                    pe.wait_ge(pq_out, n - 1)
                project(U_PQ + n, n % 2, h_from=DC if n == 0 else None)
                if n >= 1:
                    score(n - 1)
            score(N_PQ - 1)

            for tt in range(TT):
                for k in range(3):
                    pe.wait_ge(chosen_ready, 3 * tt + k + 1)
                    nc.tensor.transpose(psum[4 + k][:, tt * P:(tt + 1) * P], chosen[:, k, :], ident[:]).then_inc(chT_ready, 1)

            pe.wait_ge(chT_out, 3)

            def gates_of(i, peeled):
                for half in range(2):
                    for k in range(GSUB):
                        t = half * GSUB + k
                        if k == 0 and not peeled:
                            pe.wait_ge(set_out, 2 * i + (half - 1))
                        pe.wait_ge(hot_ready, 2 * GSUB * i + t + 1)
                        for part in range(3):
                            last = nc.tensor.matmul(psum[4 * half + k // 4][:, (k % 4) * NK:(k % 4 + 1) * NK],
                                                    hot[:, k % 4, 0, :], hot[:, k % 4, 1 + part, :],
                                                    start=part == 0, stop=part == 2)
                        last.then_inc(hot_used, 1)

            gates_of(0, True)
            with pe.Fori(1, T // (2 * GSUB)) as i:
                gates_of(i, False)

            def scores_of(first_slot, unit0, group, blocks_before):
                for j in range(GB):
                    pe.wait_ge(lo_done, unit0 + (j + 1))
                    if blocks_before is not None:
                        pe.wait_ge(w_done, blocks_before + (j + 1))
                    for c in range(DC):
                        last = three(psum[j][:], wh[:, first_slot + j, c * P:(c + 1) * P], wl[:, first_slot + j, c * P:(c + 1) * P],
                                     hh[:, c, :], hl[:, c, :], c == 0, c == DC - 1)
                    last.then_inc(unit_used, 1)

            def values_of(first_slot, unit0, parity, blocks, outs_before):
                pe.wait_ge(lo_done, unit0 + GB)
                pe.wait_ge(wsplit, blocks)
                for dc in range(DC):
                    if outs_before is not None or dc >= 4:
                        pe.wait_ge(o_out, (0 if outs_before is None else outs_before) + (dc - 3))
                    for j in range(GB):
                        last = three(psum[4 + dc % 4][:], wh[:, first_slot + j, dc * P:(dc + 1) * P],
                                     wl[:, first_slot + j, dc * P:(dc + 1) * P],
                                     act_h[:, parity, j, :], act_l[:, parity, j, :], j == 0, j == GB - 1)
                        if dc == DC - 1:
                            last.then_inc(unit_used, 1)
                    if dc < DC - 1:
                        last.then_inc(o_ready, 1)

            pe.wait_ge(set_out, T // GSUB)
            scores_of(0, U_DENSE, 0, None)
            scores_of(4, U_DENSE + GB, 1, 0)
            values_of(0, U_DENSE + 2 * GB, 0, GB, None)
            with pe.Fori(0, (GROUPS - 2) // 2) as i:
                for q in range(2):
                    scores_of(4, U_DENSE + GB * (3 + 2 * q) + 16 * i, q, GB * (1 + q) + 8 * i)
                    values_of(0, U_DENSE + GB * (4 + 2 * q) + 16 * i, (1 + q) % 2, GB * (2 + q) + 8 * i, DC * (1 + q) + 16 * i)
            values_of(4, U_PLE - GB, (GROUPS - 1) % 2, NK, DC * (GROUPS - 1))

            pe.wait_ge(w_done, NK)
            norm_sums(2, sq2)
            pe.wait_ge(pp_split, 4)
            pe.wait_ge(o_out, DC * GROUPS)
            for half in range(2):
                emb = U_PLE + 5 * half
                pe.wait_ge(lo_done, emb + 1)
                for k4 in range(4):
                    if half == 1:
                        pe.wait_ge(ple_out, k4 + 1)
                    for k in range(2):
                        last = three(psum[2 + k4][:], w(wh, emb, 2 * k4 + k), w(wl, emb, 2 * k4 + k),
                                     pt_h[:, k, :], pt_l[:, k, :], k == 0, k == 1)
                last.then_inc(unit_used, 1)
                for k4 in range(4):
                    dc = 4 * half + k4
                    if dc >= 2:
                        pe.wait_ge(ple_out, dc - 1)
                    project(emb + 1 + k4, dc % 2, h_from=2 * DC if dc == 0 else None)
            norm_sums(3, sq2)

        @block.scalar
        def _(act):
            for i in range(2):
                act.dma_start(x[:, 4 * i:4 * i + 4, :], xT[4 * i:4 * i + 4].rearrange("c p t -> p c t")).then_inc(x_in[i], 16)
            for dst, src in ((gain, gains), (wf, w_f), (bfb, b_f), (convw, conv_w)):
                act.dma_start(dst[:], src).then_inc(const_in, 16)

            def norm(k, sqb, hfb, x_sem, x_base):
                for c in range(DC):
                    if c >= 2:
                        act.wait_ge(sq_used, DC * k + c - 1)
                    if k == 0:
                        act.wait_ge(x_in[c // 4], 16)
                    else:
                        act.wait_ge(x_sem, x_base + c + 1)
                    nc.scalar.activation(sqb[:, c % 2, :], x[:, c, :], ACT.Square).then_inc(sq_ready, 1)
                act.wait_ge(var_ready, k + 1)
                nc.scalar.activation(rstd[:], rstd[:], ACT.Sqrt).then_inc(std_ready, 1)
                if k < 3:
                    for c in range(DC):
                        act.wait_ge(hf_ready, DC * k + c + 1)
                        nc.scalar.activation(hh[:, c, :], hfb[:, c % 2, :], ACT.Copy).then_inc(hh_ready, 1)

            norm(0, sq, hf, None, 0)
            act.wait_ge(unit_used, U_V + 4)
            for tt in range(TT):
                last = nc.scalar.activation(v_sb[:, tt, :], psum[tt][:], ACT.Copy)
            last.then_inc(v_out, 1)
            act.wait_ge(f_abs, 1)
            nc.scalar.activation(fe[:], fa[:], ACT.Exp, scale=-1.0).then_inc(f_exp, 1)
            act.wait_ge(f_exp, 1)
            nc.scalar.activation(fa[:], fe[:], ACT.Ln, bias=ones[:, 0:1]).then_inc(f_ln, 1)

            def gate_rows(pair):
                if pair == 0:
                    act.wait_ge(cum_out, 2)
                if pair >= 2:
                    act.wait_ge(logits_ready, 2 * TT * (pair - 1))
                for e, (rq, rk) in enumerate(((HD, HD + 1), (0, 1))):
                    h = 2 * pair + e
                    act.dma_start(qa[rq:rq + 1, pair % 2, e, :], cum[h:h + 1, :]).then_inc(aug_in[pair % 2], 16)
                    act.dma_start(ka[rk:rk + 1, pair % 2, e, :], ncum[h:h + 1, :]).then_inc(aug_in[pair % 2], 16)

            def mix_out(m):
                act.wait_ge(unit_used, U_MIX + m + 1)
                kind = MIX[m]
                pair = (m + 2) // 5 if kind in "qk" else (m - 2) // 5
                if kind == "C":
                    if pair >= 1:
                        act.wait_ge(mix_dve, 2 * pair)
                    nc.scalar.activation(c_in, psum[m % 3][:], ACT.Copy).then_inc(mix_act, 1)
                    return
                dst = qa if kind == "q" else ka
                scale = HD ** -0.5 if kind == "q" else 1.0
                if m == 0:
                    act.wait_ge(rows_ready, 1)
                if pair >= 2:
                    act.wait_ge(logits_ready, 2 * TT * (pair - 1))
                for e in range(2):
                    r = slice(HD * e, HD * (e + 1))
                    last = nc.scalar.activation(dst[r, pair % 2, e, :], psum[m % 3][r, :], ACT.Copy, scale=scale)
                last.then_inc(mix_act, 1)

            mix_out(0)
            mix_out(1)
            gate_rows(0)
            gate_rows(1)

            def probs_out(g):
                act.wait_ge(pT_ready, g + 1)
                if g >= 1:
                    act.wait_ge(pv_done, g)
                qi = g % TT
                nc.scalar.activation(probsT[:, 0:(qi + 1) * P], psum[5][:, 0:(qi + 1) * P], ACT.Copy).then_inc(pT_out, 1)

            m = 2
            for pair in range(PAIRS):
                units = 5 if pair < PAIRS - 1 else 3
                steps = units * DC
                for s in range(2 * TT):
                    for k in range(steps * s // (2 * TT), steps * (s + 1) // (2 * TT)):
                        mu = m + k // DC
                        if k % DC == DC - 1 and MIX[mu] in "qkC":
                            if MIX[mu] == "q" and pair >= 1:
                                gate_rows(pair + 1)
                            mix_out(mu)
                    g = 2 * TT * pair + s
                    qi = s % TT
                    act.wait_ge(max_ready, g + 1)
                    if g >= 2:
                        act.wait_ge(pT_ready, g - 1)
                    nc.scalar.activation(probs[:, g % 2, 0:(qi + 1) * P], psum[3 + g % 2][:, 0:(qi + 1) * P], ACT.Exp,
                                         bias=nmax[:, g % 2:g % 2 + 1],
                                         accum_out=rsum[:, g % 2:g % 2 + 1]).then_inc(exp_done, 1)
                    if g >= 1:
                        probs_out(g - 1)
                m += units
            probs_out(2 * TT * PAIRS - 1)

            for dc in range(DC):
                b = 4 * (dc % 2)
                for k, buf in enumerate((sig_a, sig_c)):
                    act.wait_ge(unit_used, U_MERGE + 3 * dc + k + 1)
                    if dc >= 2:
                        act.wait_ge(mg_out, dc - 1)
                    elif dc == 0:
                        act.wait_ge(pv_done, 2 * TT * PAIRS)
                        act.wait_ge(mix_dve, by_dve(len(MIX)))
                    nc.scalar.activation(buf[:, dc % 2, :], psum[b + k][:], ACT.Sigmoid).then_inc(sig_done, 1)
            for c in range(DC):
                if c == 0:
                    act.wait_ge(unit_used, U_OUT)
                act.wait_ge(mg_out, c + 1)
                nc.scalar.activation(hh[:, c, :], merged[:, c, :], ACT.Copy).then_inc(mh_ready, 1)

            norm(1, sq1, hf1, wo_out, 0)
            act.wait_ge(unit_used, U_OUT + DC)
            act.dma_start(keys[:], keysT).then_inc(keys_in, 16)

            def score_out(n):
                act.wait_ge(sc_ready, n + 1)
                nc.scalar.activation(scores[:, :, n, :], psum[2 + n % 2][:].rearrange("p (t n) -> p t n", t=TT),
                                     ACT.Copy).then_inc(sc_out, 1)

            for n in range(N_PQ):
                act.wait_ge(unit_used, U_PQ + n + 1)
                if n >= 2:
                    act.wait_ge(sc_ready, n - 1)
                nc.scalar.activation(qT[:, n % 2, :], psum[n % 2][:], ACT.Copy).then_inc(pq_out, 1)
                if n >= 1:
                    score_out(n - 1)
            score_out(N_PQ - 1)
            for tt in range(TT):
                act.wait_ge(top_ready, tt + 1)
                nc.scalar.activation(top[:], top[:], ACT.Exp).then_inc(gexp, 1)

            act.wait_ge(parts_ready, 1)
            sets = GT // GSUB

            def stage_chunk(i, before):
                for k in range(sets):
                    act.wait_ge(hot_used, GT * i + GSUB * (k + 1))
                    if k == 0 and before is not None:
                        act.wait_ge(gate_stored, before)
                    for b in range(4):
                        last = nc.scalar.activation(
                            stage[:, :, k * GSUB + 4 * b:k * GSUB + 4 * b + 4].rearrange("p a t -> p t a"),
                            psum[4 * (k % 2) + b][:].rearrange("p (t a) -> p t a", t=4), ACT.Copy)
                    last.then_inc(set_out, 1)
                act.wait_ge(set_out, sets * i + sets)
                act.dma_start(gate_dram[:, :, bass.ds(GT * i, GT)].rearrange("a b t -> b a t"),
                              stage[:]).then_inc(gate_stored, 16)

            stage_chunk(0, None)
            with act.Fori(1, T // GT) as i:
                stage_chunk(i, 16 * i)
            act.wait_ge(gate_stored, 16 * (T // GT))

            def load_gates(parity, group):
                src = gate_dram[group] if not isinstance(group, int) else gate_dram[GB * group:GB * group + GB]
                act.dma_start(gate[:, parity, :, :], src.rearrange("a b t -> b a t")).then_inc(gate_in[parity], 16)

            def gelus(unit0):
                for j in range(GB):
                    act.wait_ge(unit_used, unit0 + (j + 1))
                    nc.scalar.activation(psum[j][:], psum[j][:], ACT.Gelu).then_inc(gelu_done, 1)

            load_gates(0, 0)
            load_gates(1, 1)
            gelus(U_DENSE)
            gelus(U_DENSE + GB)
            with act.Fori(0, (GROUPS - 2) // 2) as i:
                for q in range(2):
                    act.wait_ge(w_done, GB * (1 + q) + 8 * i)
                    load_gates(q, bass.ds(GB * (2 + q) + 8 * i, GB))
                    gelus(U_DENSE + GB * (3 + 2 * q) + 16 * i)

            act.wait_ge(w_done, NK)
            act.dma_start(pt[:], pT).then_inc(p_in, 16)
            norm(2, sq2, hf2, o_out, DC * (GROUPS - 1))
            for dc in range(DC):
                act.wait_ge(unit_used, U_PLE + 5 * (dc // 4) + dc % 4 + 2)
                if dc >= 2:
                    act.wait_ge(ple_out, dc - 1)
                nc.scalar.activation(sg[:, dc % 2, :], psum[dc % 2][:], ACT.Sigmoid).then_inc(ple_sig, 1)
            norm(3, sq2, None, ple_out, 0)

        @block.vector
        def _(dve):
            chain = [0]

            def mark(ins):
                chain[0] += 1
                ins.then_inc(dve_own, 1)

            def link(ins):
                mark(ins)
                dve.wait_ge(dve_own, chain[0])

            def norm(k, hfb):
                dve.wait_ge(sq_used, DC * (k + 1))
                nc.vector.tensor_scalar(rstd[:], psum[NORM_BANK[k]][:], 1.0 / D, EPS, ALU.mult, ALU.add).then_inc(var_ready, 1)
                dve.wait_ge(std_ready, k + 1)
                link(nc.vector.reciprocal(rstd[:], rstd[:]))
                if k == 3:
                    for c in range(DC):
                        nc.vector.scalar_tensor_tensor(out=outb[:, c, :], in0=x[:, c, :], scalar=gain[:, k, c:c + 1],
                                                       in1=rstd[:], op0=ALU.mult, op1=ALU.mult).then_inc(out_ready, 1)
                    return
                for c in range(DC + 1):
                    if c < DC:
                        if c >= 2:
                            dve.wait_ge(h_ready, DC * k + c - 1)
                        nc.vector.scalar_tensor_tensor(out=hfb[:, c % 2, :], in0=x[:, c, :], scalar=gain[:, k, c:c + 1],
                                                       in1=rstd[:], op0=ALU.mult, op1=ALU.mult).then_inc(hf_ready, 1)
                    if c >= 1:
                        dve.wait_ge(hf_ready, DC * k + c)
                        dve.wait_ge(hh_ready, DC * k + c)
                        nc.vector.tensor_tensor(hl[:, c - 1, :], hfb[:, (c - 1) % 2, :], hh[:, c - 1, :].bitcast(F32),
                                                ALU.subtract).then_inc(h_ready, 1)

            link(nc.vector.memset(qa[0:HD, :, 1, :], 0.0))
            link(nc.vector.memset(ka[0:HD, :, 1, :], 0.0))
            nc.vector.memset(qa[0:2, :, 1, :], 1.0)
            nc.vector.memset(ka[0:2, :, 1, :], 1.0)
            nc.vector.memset(qa[HD:HD + 2, :, 0, :], 1.0)
            nc.vector.memset(z[:, 0:TAPS - 1], 0.0)
            link(nc.vector.memset(ka[HD:HD + 2, :, 0, :], 1.0))
            dve.wait_ge(const_in, 64)
            link(nc.vector.tensor_copy(wf_h[:], wf[:]))
            link(nc.vector.tensor_tensor(wf_l[:], wf[:], wf_h[:].bitcast(F32), ALU.subtract))
            nc.vector.memset(nmax[:], 0.0).then_inc(rows_ready, 1)
            norm(0, hf)

            dve.wait_ge(f_ready, 1)
            link(nc.vector.tensor_tensor(fz[:], psum[4][:, 0:TT * HEADS].rearrange("p (t h) -> p t h", t=TT),
                                         bfb[:].unsqueeze(1).to_broadcast([P, TT, HEADS]), ALU.add))
            link(nc.vector.tensor_scalar(fe[:], fz[:], -1.0, None, ALU.mult))
            nc.vector.tensor_tensor(fa[:], fz[:], fe[:], ALU.max).then_inc(f_abs, 1)
            link(nc.vector.tensor_scalar(fz[:], fz[:], 0.0, None, ALU.min))
            dve.wait_ge(f_ln, 1)
            nc.vector.tensor_tensor(logf[:], fz[:], fa[:], ALU.subtract).then_inc(logf_ready, 1)
            dve.wait_ge(cum_ready, 1)
            nc.vector.tensor_copy(cum[:], psum[5][0:HEADS, :]).then_inc(cum_out, 1)
            nc.vector.tensor_scalar(ncum[:], psum[5][0:HEADS, :], -1.0, None, ALU.mult).then_inc(cum_out, 1)

            def mix_out(m):
                kind, pair = MIX[m], (m - 2) // 5
                dve.wait_ge(unit_used, U_MIX + m + 1)
                if kind == "x":
                    dve.wait_ge(mix_act, by_act(m))
                    nc.vector.tensor_tensor(z[:, TAPS - 1:], psum[m % 3][:], c_in, ALU.mult).then_inc(mix_dve, 1)
                    dve.wait_ge(mix_dve, by_dve(m) + 1)
                    link(nc.vector.tensor_scalar(cv, z[:, 2:2 + T], convw[:, 2, pair:pair + 1], None, ALU.mult))
                    for tap in (1, 0):
                        link(nc.vector.scalar_tensor_tensor(out=cv, in0=z[:, tap:tap + T], scalar=convw[:, tap, pair:pair + 1],
                                                            in1=cv, op0=ALU.mult, op1=ALU.add))
                    return
                nc.vector.tensor_tensor(cv, psum[m % 3][:], cv, ALU.mult).then_inc(mix_dve, 1)
                dve.wait_ge(mix_dve, by_dve(m) + 1)
                link(nc.vector.tensor_copy(conv_h[:, pair, :], cv))
                link(nc.vector.tensor_tensor(conv_l[:, pair, :], cv, conv_h[:, pair, :].bitcast(F32), ALU.subtract))

            def pair_done(pair):
                dve.wait_ge(pv_done, 2 * TT * (pair + 1))
                bank = psum[6 + pair % 2]
                link(nc.vector.tensor_copy(attn_h[:, pair, :], bank[:]))
                nc.vector.tensor_tensor(attn_l[:, pair, :], bank[:], attn_h[:, pair, :].bitcast(F32),
                                        ALU.subtract).then_inc(pair_out, 1)

            m = 2
            for pair in range(PAIRS):
                units = 5 if pair < PAIRS - 1 else 3
                steps = units * DC
                for s in range(2 * TT):
                    for k in range(steps * s // (2 * TT), steps * (s + 1) // (2 * TT)):
                        mu = m + k // DC
                        if k % DC == DC - 1 and MIX[mu] in "xB":
                            mix_out(mu)
                    g = 2 * TT * pair + s
                    qi = s % TT
                    bank = psum[3 + g % 2]
                    diag = bank[:, qi * P:(qi + 1) * P]
                    dve.wait_ge(logits_ready, g + 1)
                    link(nc.vector.tensor_tensor(diag, diag, mask[:], ALU.add))
                    nc.vector.tensor_reduce(nmax[:, g % 2:g % 2 + 1], bank[:, 0:(qi + 1) * P], AX.X, ALU.max,
                                            negate=True).then_inc(max_ready, 1)
                    dve.wait_ge(exp_done, g + 1)
                    link(nc.vector.reciprocal(rsum[:, g % 2:g % 2 + 1], rsum[:, g % 2:g % 2 + 1]))
                    row = probs[:, g % 2, 0:(qi + 1) * P]
                    nc.vector.tensor_scalar(row, row, rsum[:, g % 2:g % 2 + 1], None, ALU.mult).then_inc(probs_ready, 1)
                    if pair >= 1 and s == 2:
                        pair_done(pair - 1)
                m += units
            pair_done(PAIRS - 1)

            for dc in range(DC):
                b = 4 * (dc % 2)
                dve.wait_ge(unit_used, U_MERGE + 3 * dc + 3)
                dve.wait_ge(sig_done, 2 * dc + 2)
                mark(nc.vector.tensor_tensor(sig_a[:, dc % 2, :], psum[b + 2][:], sig_a[:, dc % 2, :], ALU.mult))
                link(nc.vector.tensor_tensor(sig_c[:, dc % 2, :], psum[b + 3][:], sig_c[:, dc % 2, :], ALU.mult))
                nc.vector.tensor_tensor(merged[:, dc, :], sig_a[:, dc % 2, :], sig_c[:, dc % 2, :], ALU.add).then_inc(mg_out, 1)
            for c in range(DC):
                dve.wait_ge(mg_out, c + 1)
                dve.wait_ge(mh_ready, c + 1)
                nc.vector.tensor_tensor(hl[:, c, :], merged[:, c, :], hh[:, c, :].bitcast(F32), ALU.subtract).then_inc(ml_ready, 1)
            for dc in range(DC):
                dve.wait_ge(unit_used, U_OUT + dc + 1)
                nc.vector.tensor_tensor(x[:, dc, :], psum[dc % 4][:], x[:, dc, :], ALU.add).then_inc(wo_out, 1)
            norm(1, hf1)

            def best(values, vals, idx):
                link(nc.vector.max(vals[:, 0:8], values))
                link(nc.vector.max_index(idx[:, 0:8], vals[:, 0:8], values))
                link(nc.vector.match_replace(values, vals[:, 0:8], values, MASKED))
                link(nc.vector.max(vals[:, 8:16], values))
                link(nc.vector.max_index(idx[:, 8:16], vals[:, 8:16], values))

            for tt in range(TT):
                dve.wait_ge(sc_out, N_PQ)
                for n in range(N_PQ):
                    best(scores[:, tt, n, :], v12[:, n, :], i12[:, n, :])
                vv = v12[:].rearrange("p (h s) k -> p h s k", s=2)
                link(nc.vector.tensor_tensor(cand[:], vv[:, :, 0, :].unsqueeze(3).to_broadcast([P, PH, TOPK, TOPK]),
                                             vv[:, :, 1, :].unsqueeze(2).to_broadcast([P, PH, TOPK, TOPK]), ALU.add))
                for h in range(PH):
                    best(cand[:, h, :, :].rearrange("p a b -> p (a b)"), top[:, h, :], topj[:, h, :])
                tj = topj[:].rearrange("p h k -> p (h k)")
                nc.vector.tensor_scalar(rank[:, 0, :], tj, 4, None, ALU.logical_shift_right)
                link(nc.vector.tensor_scalar(rank[:, 1, :], tj, TOPK - 1, None, ALU.bitwise_and))
                nc.vector.tensor_copy(rankb[:], rank[:])
                link(nc.vector.tensor_copy(i12b[:], i12[:]))
                link(nc.vector.tensor_copy(gsum[:, 1, :], top[:, :, 0]))
                nc.vector.tensor_tensor(top[:], top[:], gsum[:, 1, :].unsqueeze(2).to_broadcast([P, PH, TOPK]),
                                        ALU.subtract).then_inc(top_ready, 1)
                ii = i12b[:].rearrange("p (h s) k -> p h s k", s=2)
                for side in range(2):
                    base = (tt * N_PQ * NK) * 2
                    sel = oh[:, base:base + HK * TOPK].rearrange("p (c r) -> p c r", r=TOPK)
                    if side == 0 and tt > 0:
                        dve.wait_ge(chT_ready, 3 * tt)
                    elif side == 1:
                        dve.wait_ge(chosen_ready, 3 * tt + 1)
                    link(nc.vector.tensor_tensor(sel, rankb[:, side, :].unsqueeze(2).to_broadcast([P, HK, TOPK]),
                                                 iota_k[:].unsqueeze(1).to_broadcast([P, HK, TOPK]), ALU.is_equal))
                    sel4 = sel.rearrange("p (h k) r -> p h k r", h=PH)
                    link(nc.vector.tensor_tensor(sel4, sel4, ii[:, :, side, :].unsqueeze(2).to_broadcast([P, PH, TOPK, TOPK]),
                                                 ALU.mult))
                    nc.vector.tensor_reduce(chosen[:, side, :], sel, AX.X, ALU.add).then_inc(chosen_ready, 1)
                dve.wait_ge(gexp, tt + 1)
                link(nc.vector.tensor_reduce(gsum[:, 0, :], top[:], AX.X, ALU.add))
                link(nc.vector.reciprocal(gsum[:, 0, :], gsum[:, 0, :]))
                nc.vector.tensor_tensor(chosen[:, 2, :].rearrange("p (h k) -> p h k", h=PH), top[:],
                                        gsum[:, 0, :].unsqueeze(2).to_broadcast([P, PH, TOPK]),
                                        ALU.mult).then_inc(chosen_ready, 1)
            dve.wait_ge(chT_ready, 3 * TT)
            nc.vector.tensor_copy(i1T[:], psum[4][:]).then_inc(chT_out, 1)
            nc.vector.tensor_copy(i2T[:], psum[5][:]).then_inc(chT_out, 1)
            nc.vector.tensor_copy(gT, psum[6][:]).then_inc(chT_out, 1)
            dve.wait_ge(chT_out, 3)
            for part in (g1, g2, g3):
                link(nc.vector.tensor_copy(gb[:], gT))
                link(nc.vector.tensor_copy(part[:], gb[:]))
                link(nc.vector.tensor_tensor(gT, gT, part[:], ALU.subtract))
            nc.vector.memset(gb[:], 0.0).then_inc(parts_ready, 1)

            def one_hots(k, t, before):
                if before is not None:
                    dve.wait_ge(hot_used, before)
                at = bass.ds(t, 1)
                nc.vector.tensor_scalar(hot[:, k % 4, 0, :], iota_nk[:], i2T[:, at], None, ALU.is_equal)
                for part, gp in enumerate((g1, g2, g3)):
                    last = nc.vector.tensor_scalar(hot[:, k % 4, 1 + part, :], iota_nk[:], i1T[:, at], gp[:, at],
                                                   ALU.is_equal, ALU.mult)
                last.then_inc(hot_ready, 1)

            for k in range(GSUB):
                one_hots(k, k, k - 3 if k >= 4 else None)
            with dve.Fori(1, T // GSUB) as i:
                for k in range(GSUB):
                    one_hots(k, GSUB * i + k, GSUB * i + (k - 3))

            def weigh(parity, blocks, gate_turn):
                for j in range(GB):
                    dve.wait_ge(gelu_done, blocks + (j + 1))
                    if j == 0:
                        dve.wait_ge(gate_in[parity], gate_turn)
                    nc.vector.tensor_tensor(wt[:, j % 2, :], psum[j][:], gate[:, parity, j, :], ALU.mult).then_inc(w_done, 1)
                    dve.wait_ge(w_done, blocks + (j + 1))
                    nc.vector.tensor_copy(act_h[:, parity, j, :], wt[:, j % 2, :]).then_inc(wcopy, 1)
                    dve.wait_ge(wcopy, blocks + (j + 1))
                    nc.vector.tensor_tensor(act_l[:, parity, j, :], wt[:, j % 2, :], act_h[:, parity, j, :].bitcast(F32),
                                            ALU.subtract).then_inc(wsplit, 1)

            def add_values(outs, unit0):
                for dc in range(DC):
                    if dc < DC - 1:
                        dve.wait_ge(o_ready, outs + (dc + 1))
                    else:
                        dve.wait_ge(unit_used, unit0 + GB)
                    nc.vector.tensor_tensor(x[:, dc, :], psum[4 + dc % 4][:], x[:, dc, :], ALU.add).then_inc(o_out, 1)

            weigh(0, 0, 16)
            weigh(1, GB, 16)
            add_values(0, U_DENSE + 2 * GB)
            with dve.Fori(0, (GROUPS - 2) // 2) as i:
                for q in range(2):
                    weigh(q, GB * (2 + q) + 8 * i, 32 + 16 * i)
                    add_values((DC - 1) * (1 + q) + 14 * i, U_DENSE + GB * (4 + 2 * q) + 16 * i)
            add_values((DC - 1) * (GROUPS - 1), U_PLE - GB)

            dve.wait_ge(p_in, 16)
            for k in range(2):
                nc.vector.tensor_copy(pt_h[:, k, :], pt[:, k, :]).then_inc(pp_split, 1)
                dve.wait_ge(pp_split, 2 * k + 1)
                nc.vector.tensor_tensor(pt_l[:, k, :], pt[:, k, :], pt_h[:, k, :].bitcast(F32), ALU.subtract).then_inc(pp_split, 1)
            norm(2, hf2)
            for dc in range(DC):
                dve.wait_ge(ple_sig, dc + 1)
                link(nc.vector.tensor_tensor(upd[:, dc % 2, :], psum[2 + dc % 4][:], sg[:, dc % 2, :], ALU.mult))
                nc.vector.tensor_tensor(x[:, dc, :], x[:, dc, :], upd[:, dc % 2, :], ALU.add).then_inc(ple_out, 1)
            norm(3, None)


def weight_stream(np, w_in, w_branch, w_out, w_peer_q, peer_u, peer_v, w_ple_gate, w_ple_proj):
    def tiles(w):
        k, n = w.shape
        return w.reshape(k // P, P, n // P, P).transpose(2, 1, 0, 3).reshape(n // P, P, -1)

    q, k, v, _, B, C, xc, ga, gc = np.split(w_in, np.cumsum([CW, CW, CW, HEADS, CW, CW, CW, D]), axis=1)
    vt = v.reshape(4, 2, P, CW).transpose(0, 2, 1, 3).reshape(4, P, UW)
    parts = {n: tiles(a) for n, a in (("q", q), ("k", k), ("C", C), ("x", xc), ("B", B))}
    at = dict.fromkeys(parts, 0)
    units = list(vt)
    for kind in MIX:
        units.append(parts[kind][at[kind]])
        at[kind] += 1
    ga, gc = tiles(ga), tiles(gc)
    branches = np.concatenate([tiles(w_branch[0]), tiles(w_branch[1])], axis=2)
    for dc in range(DC):
        units += [ga[dc], gc[dc], branches[dc]]
    units += list(tiles(w_out))
    units += list(tiles(w_peer_q.reshape(D, N_PQ * P)))
    u = peer_u.reshape(NK, NK, DC, P).transpose(0, 3, 2, 1).reshape(NK, P, UW)
    v = peer_v.reshape(NK, NK, D)
    groups = [slice(GB * g, GB * g + GB) for g in range(GROUPS)]
    units += list(u[groups[0]])
    for g in range(1, GROUPS):
        units += list(u[groups[g]]) + list(v[groups[g - 1]])
    units += list(v[groups[-1]])
    gate = tiles(w_ple_gate)
    emb = w_ple_proj.reshape(2, P, 2, 4, P).transpose(2, 1, 3, 0, 4).reshape(2, P, UW)
    for half in range(2):
        units += [emb[half]] + list(gate[4 * half:4 * half + 4])
    return np.stack(units)


def kernel(**inputs):
    import numpy as np
    import concourse.bacc as bacc
    from concourse.bass_utils import run_bass_kernel_spmd

    a = {n: np.asarray(v) for n, v in inputs.items()}
    w_in = a["w_in"][0]
    arrays = {
        "xT": a["x"][0].T.reshape(DC, P, T),
        "pT": a["p"][0, 0].T.reshape(2, P, T).transpose(1, 0, 2),
        "stream": weight_stream(np, w_in, a["w_branch"][0], a["w_out"][0], a["w_peer_q"][0], a["peer_u"][0],
                                a["peer_v"][0], a["w_ple_gate"][0], a["w_ple_proj"][0]),
        "w_f": w_in[:, 3 * CW:3 * CW + HEADS].reshape(DC, P, HEADS).transpose(1, 0, 2),
        "b_f": np.broadcast_to(a["b_f"][0], (P, HEADS)),
        "conv_w": a["conv_w"][0].reshape(TAPS, CC, P).transpose(2, 0, 1),
        "gains": np.stack([a["g_mix"][0], a["g_ffn"][0], a["g_ple"][0], a["g_final"]]).reshape(4, DC, P).transpose(2, 0, 1),
        "keysT": np.stack([a["peer_k1"][0], a["peer_k2"][0]], axis=1).reshape(N_PQ, NK, P).transpose(2, 0, 1),
    }
    arrays = {n: np.ascontiguousarray(v) for n, v in arrays.items()}
    nc = bacc.Bacc("TRN2", target_bir_lowering=False, num_devices=1)
    args = {n: nc.dram_tensor(n, v.shape, mybir.dt.from_np(v.dtype), kind="ExternalInput").ap() for n, v in arrays.items()}
    gate_dram = nc.dram_tensor("gate_dram", (NK, NK, T), F32, kind="Internal").ap()
    outT = nc.dram_tensor("outT", (DC, P, T), F32, kind="ExternalOutput").ap()
    peer_block_kernel(nc, gate_dram=gate_dram, outT=outT, **args)
    r = run_bass_kernel_spmd(nc, [arrays], core_ids=[0])
    return r.results[0]["outT"].reshape(D, T).T.reshape(1, T, D)
```

```python
from contextlib import ExitStack

import concourse.bass as bass
from concourse import mybir

F32 = mybir.dt.float32
F32R = mybir.dt.float32r
BF16 = mybir.dt.bfloat16
U32 = mybir.dt.uint32
ALU = mybir.AluOpType
ACT = mybir.ActivationFunctionType
AX = mybir.AxisListType

P = 128
T = 512
TT = T // P
D = 1024
DC = D // P
HEADS = 8
PAIRS = HEADS // 2
HD = 64
CW = 512
CC = CW // P
TAPS = 3
PH = 8
NK = 128
TOPK = 16
HK = PH * TOPK
CAND = TOPK * TOPK
PLE = 256
EPS = 1e-6
NORM_BANK = (7, 7, 1, 7)
MASKED = -3.0e38

UW = 1024
U_V = 0
U_MIX = U_V + 4
N_MIX = 5 * PAIRS
U_MERGE = U_MIX + N_MIX
N_MERGE = 3 * DC
U_OUT = U_MERGE + N_MERGE
U_PQ = U_OUT + DC
N_PQ = 2 * PH
U_DENSE = U_PQ + N_PQ
GB = 4
GROUPS = NK // GB
ROUTE_U = 24
GATE_U = 8
EARLY = (ROUTE_U + GATE_U * TT) // GB
U_GATE = U_DENSE + ROUTE_U
U_S0 = U_GATE + GATE_U * TT
U_V0 = U_S0 + GB
U_SV = U_V0 + GB * EARLY
U_PLE = U_DENSE + 2 * NK
N_UNITS = U_PLE + DC + 2
RAW = 4
SL = 8

MIX = ["q", "k"]
for _i in range(PAIRS):
    MIX += ["C", "x", "B"] + (["q", "k"] if _i < PAIRS - 1 else [])

GT = 32
CH = T // GT
HB = 8
QUAD = 4
EXP_AT = (7, 13, 18, 23)
CHOSEN_AT = (9, 15, 20, 24)


def peer_block_kernel(nc, xT, pT, stream, w_f, b_f, conv_w, gains, keysT, gate_dram, gelu_dram, outT):
    ctx = ExitStack()
    with ctx:
        def sb(name, shape, dt, where=ctx):
            return where.enter_context(nc.sbuf_tensor(name, shape, dt))

        def sem(name):
            return ctx.enter_context(nc.semaphore(name))

        x = sb("x", [P, DC, T], F32)
        hh = sb("hh", [P, DC, T], F32R)
        hl = sb("hl", [P, DC, T], F32R)
        raw = sb("raw", [P, RAW, UW], F32)
        wh = sb("wh", [P, SL, UW], F32R)
        wl = sb("wl", [P, SL, UW], F32R)
        ones = sb("ones", [P, P], F32)
        ident = sb("ident", [P, P], F32)
        iota_nk = sb("iota_nk", [P, NK], F32)
        iota_k = sb("iota_k", [P, TOPK], BF16)
        gain = sb("gain", [P, 4, DC], F32)
        rstd = sb("rstd", [P, T], F32)

        mix = ExitStack()
        sq = sb("sq", [P, 2, T], F32, mix)
        hf = sb("hf", [P, 2, T], F32, mix)
        attn_h = sb("attn_h", [P, CC, T], F32R, mix)
        attn_l = sb("attn_l", [P, CC, T], F32R, mix)
        conv_h = sb("conv_h", [P, CC, T], F32R, mix)
        conv_l = sb("conv_l", [P, CC, T], F32R, mix)
        att = ExitStack()
        v_sb = sb("v_sb", [P, TT, CW], F32, att)
        qa = sb("qa", [P, 2, 2, T], F32, att)
        ka = sb("ka", [P, 2, 2, T], F32, att)
        probs = sq
        probsT = sb("probsT", [P, T], F32, att)
        c_in = hf[:, 1, :]
        cv = hf[:, 0, :]
        z = sb("z", [P, T + TAPS - 1], F32, att)
        tri = sb("tri", [P, T], F32, att)
        mask = sb("mask", [P, P], F32, att)
        wf = sb("wf", [P, DC, HEADS], F32, att)
        wf_h = sb("wf_h", [P, DC, HEADS], F32R, att)
        wf_l = sb("wf_l", [P, DC, HEADS], F32R, att)
        bfb = sb("bfb", [P, HEADS], F32, att)
        fz = sb("fz", [P, TT, HEADS], F32, att)
        fa = sb("fa", [P, TT, HEADS], F32, att)
        fe = sb("fe", [P, TT, HEADS], F32, att)
        logf = sb("logf", [P, TT, HEADS], F32, att)
        cum = sb("cum", [HEADS, T], F32, att)
        ncum = sb("ncum", [HEADS, T], F32, att)
        convw = sb("convw", [P, TAPS, CC], F32, att)
        nmax = sb("nmax", [P, 2], F32, att)
        rsum = sb("rsum", [P, 2], F32, att)
        att.close()
        mrg = ExitStack()
        merged = sb("merged", [P, DC, T], F32, mrg)
        sig_a = sb("sig_a", [P, 2, T], F32, mrg)
        sig_c = sb("sig_c", [P, 2, T], F32, mrg)
        mrg.close()
        mix.close()
        rt = ExitStack()
        sq1 = sb("sq1", [P, 2, T], F32, rt)
        hf1 = sb("hf1", [P, 2, T], F32, rt)
        i1T = sb("i1T", [P, T], F32, rt)
        i2T = sb("i2T", [P, T], F32, rt)
        gT = sb("gT", [P, T], F32, rt)
        gout = sb("gout", [P, 2, T], F32, rt)
        rs = ExitStack()
        keys = sb("keys", [P, N_PQ, NK], F32, rs)
        qT = hf1
        scores = sb("scores", [P, 2, TT, NK], F32, rs)
        cand = sb("cand", [P, PH, TOPK, TOPK], F32, rs)
        v12 = sb("v12", [P, TT, N_PQ, TOPK], F32, rs)
        i12 = sb("i12", [P, TT, N_PQ, TOPK], U32, rs)
        i12b = sb("i12b", [P, N_PQ, TOPK], BF16, rs)
        top = sb("top", [P, PH, TOPK], F32, rs)
        topj = sb("topj", [P, PH, TOPK], U32, rs)
        rank = sb("rank", [P, 2, HK], U32, rs)
        rankb = sb("rankb", [P, 2, HK], BF16, rs)
        onehot = sb("onehot", [P, HK, TOPK], BF16, rs)
        gsum = sb("gsum", [P, 2, PH], F32, rs)
        chosen = sb("chosen", [P, 2, 3, HK], F32, rs)
        rs.close()
        gs = ExitStack()
        hot = sb("hot", [P, 2, 2, HB, NK], F32, gs)
        stage = sb("stage", [P, 2, NK, GT], F32, gs)
        gs.close()
        rt.close()
        ex = ExitStack()
        gate = sb("gate", [P, 2, CH, GB, GT], F32, ex)
        gelu_in = sb("gelu_in", [P, 2, GB, T], F32, ex)
        wt = sb("wt", [P, 2, T], F32, ex)
        act_h = sb("act_h", [P, 2, GB, T], F32R, ex)
        act_l = sb("act_l", [P, 2, GB, T], F32R, ex)
        ex.close()
        pl = ExitStack()
        sq2 = sb("sq2", [P, 2, T], F32, pl)
        hf2 = sb("hf2", [P, 2, T], F32, pl)
        pt = sb("pt", [P, 2, T], F32, pl)
        pt_h = sb("pt_h", [P, 2, T], F32R, pl)
        pt_l = sb("pt_l", [P, 2, T], F32R, pl)
        sg = sb("sg", [P, 2, T], F32, pl)
        upd = sb("upd", [P, 2, T], F32, pl)
        outb = sb("outb", [P, DC, T], F32, pl)
        pl.close()
        psum = [ctx.enter_context(nc.psum_tensor(f"bank{b}", [P, T], F32)) for b in range(8)]

        x_in = [sem(f"x_in{i}") for i in range(2)]
        const_in = sem("const_in")
        keys_in = sem("keys_in")
        p_in = sem("p_in")
        raw_in = [sem(f"raw_in{i}") for i in range(RAW)]
        hi_done = sem("hi_done")
        lo_done = sem("lo_done")
        unit_used = sem("unit_used")
        consts = sem("consts")
        consts2 = sem("consts2")
        sq_ready = sem("sq_ready")
        sq_used = sem("sq_used")
        var_ready = sem("var_ready")
        std_ready = sem("std_ready")
        hf_ready = sem("hf_ready")
        hh_ready = sem("hh_ready")
        h_ready = sem("h_ready")
        v_out = sem("v_out")
        f_ready = sem("f_ready")
        f_abs = sem("f_abs")
        f_exp = sem("f_exp")
        f_ln = sem("f_ln")
        logf_ready = sem("logf_ready")
        cum_ready = sem("cum_ready")
        cum_out = sem("cum_out")
        aug_in = [sem(f"aug_in{i}") for i in range(2)]
        mix_act = sem("mix_act")
        mix_dve = sem("mix_dve")
        logits_ready = sem("logits_ready")
        max_ready = sem("max_ready")
        exp_done = sem("exp_done")
        probs_ready = sem("probs_ready")
        pT_ready = sem("pT_ready")
        pT_out = sem("pT_out")
        pv_done = sem("pv_done")
        pair_out = sem("pair_out")
        sig_done = sem("sig_done")
        mg_out = sem("mg_out")
        mh_ready = sem("mh_ready")
        ml_ready = sem("ml_ready")
        wo_out = sem("wo_out")
        pq_out = sem("pq_out")
        sc_ready = sem("sc_ready")
        sc_out = sem("sc_out")
        top_ready = sem("top_ready")
        gexp = sem("gexp")
        chosen_ready = sem("chosen_ready")
        chT_ready = sem("chT_ready")
        chT_out = sem("chT_out")
        hot_ready = sem("hot_ready")
        sc_used = sem("sc_used")
        hot_own = sem("hot_own")
        quad_done = sem("quad_done")
        quad_out = sem("quad_out")
        stage_out = [sem(f"stage_out{i}") for i in range(2)]
        gelu_out = [sem(f"gelu_out{i}") for i in range(2)]
        early_done = sem("early_done")
        gelu_back = [sem(f"gelu_back{i}") for i in range(2)]
        gate_in = [sem(f"gate_in{i}") for i in range(2)]
        gelu_done = sem("gelu_done")
        wcopy = sem("wcopy")
        rows_ready = sem("rows_ready")
        w_done = sem("w_done")
        wsplit = sem("wsplit")
        o_ready = sem("o_ready")
        o_out = sem("o_out")
        pp_split = sem("pp_split")
        ple_sig = sem("ple_sig")
        ple_out = sem("ple_out")
        out_ready = sem("out_ready")
        stored = sem("stored")
        dve_own = sem("dve_own")

        block = ctx.enter_context(nc.Block())

        def by_act(m):
            return sum(k in "qkC" for k in MIX[:m])

        def by_dve(m):
            return sum(k in "xB" for k in MIX[:m])

        def wait_mix_out(eng, m):
            if MIX[m] in "qkC":
                eng.wait_ge(mix_act, by_act(m) + 1)
            else:
                eng.wait_ge(mix_dve, by_dve(m) + 1)

        @block.sync
        def _(sp):
            for n in range(SL):
                if n >= RAW:
                    sp.wait_ge(lo_done, n - RAW + 1)
                sp.dma_start(raw[:, n % RAW, :], stream[n]).then_inc(raw_in[n % RAW], 16)
            with sp.Fori(1, N_UNITS // SL) as i:
                for u in range(SL):
                    sp.wait_ge(lo_done, SL * i + (u - RAW + 1))
                    sp.dma_start(raw[:, u % RAW, :],
                                 stream[bass.ds(SL * i + u, 1)].rearrange("o p w -> p (o w)")).then_inc(raw_in[u % RAW], 16)
            for n in range(N_UNITS // SL * SL, N_UNITS):
                sp.wait_ge(lo_done, n - RAW + 1)
                sp.dma_start(raw[:, n % RAW, :], stream[n]).then_inc(raw_in[n % RAW], 16)

            for c in range(DC):
                sp.wait_ge(out_ready, c + 1)
                sp.dma_start(outT[c], outb[:, c, :]).then_inc(stored, 16)
            sp.wait_ge(stored, 16 * DC)

        @block.gpsimd
        def _(pool):
            nc.gpsimd.memset(ones[:], 1.0).then_inc(consts, 1)
            nc.gpsimd.memset(ident[:], 0.0).then_inc(consts, 1)
            nc.gpsimd.memset(tri[:], 1.0).then_inc(consts, 1)
            nc.gpsimd.memset(mask[:], 0.0).then_inc(consts, 1)
            pool.wait_ge(consts, 4)
            nc.gpsimd.affine_select(out=ident[:], in_=ident[:], compare_op=ALU.not_equal, fill=1.0, base=0,
                                    pattern=[[-1, P]], channel_multiplier=1).then_inc(consts2, 1)
            nc.gpsimd.affine_select(out=tri[:], in_=tri[:], compare_op=ALU.is_ge, fill=0.0, base=0,
                                    pattern=[[1, T]], channel_multiplier=-1).then_inc(consts2, 1)
            nc.gpsimd.affine_select(out=mask[:], in_=mask[:], compare_op=ALU.is_ge, fill=MASKED, base=0,
                                    pattern=[[-1, P]], channel_multiplier=1).then_inc(consts2, 1)
            nc.gpsimd.iota(iota_nk[:], pattern=[[1, NK]], base=0, channel_multiplier=0,
                           allow_small_or_imprecise_dtypes=True).then_inc(consts2, 1)
            nc.gpsimd.iota(iota_k[:], pattern=[[1, TOPK]], base=0, channel_multiplier=0,
                           allow_small_or_imprecise_dtypes=True).then_inc(consts2, 1)

            def low(u, unit):
                pool.wait_ge(hi_done, unit + 1)
                nc.gpsimd.tensor_tensor(wl[:, u, :], raw[:, u % RAW, :], wh[:, u, :].bitcast(F32),
                                        ALU.subtract).then_inc(lo_done, 1)

            for u in range(SL):
                low(u, u)
            with pool.Fori(1, N_UNITS // SL) as i:
                for u in range(SL):
                    low(u, SL * i + u)
            for n in range(N_UNITS // SL * SL, N_UNITS):
                low(n % SL, n)

        @block.tensor
        def _(pe):
            def three(out, ah, al, bh, bl, start, stop):
                nc.tensor.matmul(out, ah, bh, start=start, stop=False)
                nc.tensor.matmul(out, ah, bl, start=False, stop=False)
                return nc.tensor.matmul(out, al, bh, start=False, stop=stop)

            def w(part, n, c):
                return part[:, n % SL, c * P:(c + 1) * P]

            def project(n, bank, c0=0, c1=DC, h_from=None):
                for c in range(c0, c1):
                    if c == 0:
                        pe.wait_ge(lo_done, n + 1)
                    if h_from is not None:
                        pe.wait_ge(h_ready, h_from + c + 1)
                    last = three(psum[bank][:], w(wh, n, c), w(wl, n, c), hh[:, c, :], hl[:, c, :], c == 0, c == DC - 1)
                if c1 == DC:
                    last.then_inc(unit_used, 1)
                return last

            def norm_sums(k, sqb):
                for c in range(DC):
                    pe.wait_ge(sq_ready, DC * k + c + 1)
                    nc.tensor.matmul(psum[NORM_BANK[k]][:], ones[:], sqb[:, c % 2, :], start=c == 0, stop=c == DC - 1).then_inc(sq_used, 1)

            pe.wait_ge(consts2, 5)
            norm_sums(0, sq)
            for j in range(4):
                pe.wait_ge(lo_done, U_V + j + 1)
                for c in (2 * j, 2 * j + 1):
                    pe.wait_ge(h_ready, c + 1)
                    for tt in range(TT):
                        cols = slice(tt * P, (tt + 1) * P)
                        wc = slice((c % 2) * CW, (c % 2 + 1) * CW)
                        last = three(psum[tt][:], hh[:, c, cols], hl[:, c, cols], wh[:, U_V + j, wc], wl[:, U_V + j, wc],
                                     c == 0, c == DC - 1)
                last.then_inc(unit_used, 1)
            for tt in range(TT):
                cols = slice(tt * P, (tt + 1) * P)
                for c in range(DC):
                    last = three(psum[4][:, tt * HEADS:(tt + 1) * HEADS], hh[:, c, cols], hl[:, c, cols],
                                 wf_h[:, c, :], wf_l[:, c, :], c == 0, c == DC - 1)
            last.then_inc(f_ready, 1)

            pe.wait_ge(v_out, 1)
            project(U_MIX, 0)
            project(U_MIX + 1, 1)
            pe.wait_ge(logf_ready, 1)
            for j in range(TT):
                last = nc.tensor.matmul(psum[5][0:HEADS, j * P:T], logf[:, j, :], tri[:, 0:T - j * P],
                                        start=j == 0, stop=j == TT - 1)
            last.then_inc(cum_ready, 1)

            def rows(e):
                return slice(0, HD + 2) if e == 0 else slice(0, P)

            def transposes(g):
                e, qi = (g // TT) % 2, g % TT
                pe.wait_ge(probs_ready, g + 1)
                if g >= 1:
                    pe.wait_ge(pT_out, g)
                for kj in range(qi + 1):
                    last = nc.tensor.transpose(psum[5][:, kj * P:(kj + 1) * P], probs[:, g % 2, kj * P:(kj + 1) * P], ident[:])
                last.then_inc(pT_ready, 1)

            def values(g):
                pair, e, qi = g // (2 * TT), (g // TT) % 2, g % TT
                pe.wait_ge(pT_out, g + 1)
                if g % (2 * TT) == 0 and pair >= 2:
                    pe.wait_ge(pair_out, pair - 1)
                head = 2 * pair + e
                for kj in range(qi + 1):
                    last = nc.tensor.matmul(psum[6 + pair % 2][HD * e:HD * (e + 1), qi * P:(qi + 1) * P],
                                            v_sb[:, kj, head * HD:(head + 1) * HD], probsT[:, kj * P:(kj + 1) * P],
                                            start=kj == 0, stop=kj == qi)
                last.then_inc(pv_done, 1)

            m = 2
            for pair in range(PAIRS):
                units = 5 if pair < PAIRS - 1 else 3
                steps = units * DC
                for s in range(2 * TT):
                    for k in range(steps * s // (2 * TT), steps * (s + 1) // (2 * TT)):
                        mu, c = m + k // DC, k % DC
                        if c == 0 and mu >= 3:
                            wait_mix_out(pe, mu - 3)
                        last = project(U_MIX + mu, mu % 3, c, c + 1)
                    g = 2 * TT * pair + s
                    e, qi = s // TT, s % TT
                    if s == 0:
                        pe.wait_ge(aug_in[pair % 2], 64 * (pair // 2 + 1))
                        wait_mix_out(pe, 1 + 5 * pair)
                    if g >= 2:
                        pe.wait_ge(exp_done, g - 1)
                    nc.tensor.matmul(psum[3 + g % 2][:, 0:(qi + 1) * P], qa[rows(e), pair % 2, e, qi * P:(qi + 1) * P],
                                     ka[rows(e), pair % 2, e, 0:(qi + 1) * P], start=True, stop=True).then_inc(logits_ready, 1)
                    if g >= 1:
                        transposes(g - 1)
                    if g >= 2:
                        values(g - 2)
                m += units
            last_g = 2 * TT * PAIRS - 1
            transposes(last_g)
            values(last_g - 1)
            values(last_g)

            for dc in range(DC):
                n, b = U_MERGE + 3 * dc, 4 * (dc % 2)
                if dc >= 2:
                    pe.wait_ge(mg_out, dc - 1)
                elif dc == 0:
                    wait_mix_out(pe, len(MIX) - 1)
                    wait_mix_out(pe, len(MIX) - 2)
                    wait_mix_out(pe, len(MIX) - 3)
                project(n, b)
                project(n + 1, b + 1)
                pe.wait_ge(lo_done, n + 3)
                if dc == 0:
                    pe.wait_ge(pair_out, PAIRS)
                    pe.wait_ge(exp_done, 2 * TT * PAIRS)
                for br, (bh, bl) in enumerate(((attn_h, attn_l), (conv_h, conv_l))):
                    for c in range(CC):
                        last = three(psum[b + 2 + br][:], w(wh, n + 2, br * CC + c), w(wl, n + 2, br * CC + c),
                                     bh[:, c, :], bl[:, c, :], c == 0, c == CC - 1)
                last.then_inc(unit_used, 1)

            for dc in range(DC):
                if dc >= 4:
                    pe.wait_ge(wo_out, dc - 3)
                elif dc == 0:
                    pe.wait_ge(mg_out, DC)
                for c in range(DC):
                    if c == 0:
                        pe.wait_ge(lo_done, U_OUT + dc + 1)
                    if dc == 0:
                        pe.wait_ge(ml_ready, c + 1)
                    n = U_OUT + dc
                    last = three(psum[dc % 4][:], w(wh, n, c), w(wl, n, c), hh[:, c, :], hl[:, c, :], c == 0, c == DC - 1)
                last.then_inc(unit_used, 1)

            norm_sums(1, sq1)
            pe.wait_ge(keys_in, 16)

            def score(n):
                pe.wait_ge(pq_out, n + 1)
                if n >= 2:
                    pe.wait_ge(sc_out, n - 1)
                for tt in range(TT):
                    last = nc.tensor.matmul(psum[2 + n % 2][:, tt * NK:(tt + 1) * NK], qT[:, n % 2, tt * P:(tt + 1) * P],
                                            keys[:, n, :], start=True, stop=True)
                last.then_inc(sc_ready, 1)

            for n in range(N_PQ):
                if n == 0:
                    pe.wait_ge(wo_out, DC)
                if n >= 2:
                    pe.wait_ge(pq_out, n - 1)
                project(U_PQ + n, n % 2, h_from=DC if n == 0 else None)
                if n >= 1:
                    score(n - 1)
            score(N_PQ - 1)

            def block_scores(slot, lo_needed, bank, c0=0, c1=DC):
                for c in range(c0, c1):
                    if c == 0:
                        pe.wait_ge(lo_done, lo_needed)
                    cols = slice(c * P, (c + 1) * P)
                    last = three(psum[bank][:], wh[:, slot, cols], wl[:, slot, cols], hh[:, c, :], hl[:, c, :],
                                 c == 0, c == DC - 1)
                if c1 == DC:
                    last.then_inc(unit_used, 1)

            def chosen_transposed(tt):
                for k in range(3):
                    pe.wait_ge(chosen_ready, 3 * tt + k + 1)
                    nc.tensor.transpose(psum[4 + k][:, tt * P:(tt + 1) * P], chosen[:, tt % 2, k, :], ident[:]).then_inc(chT_ready, 1)

            pe.wait_ge(sc_out, N_PQ)
            for u in range(ROUTE_U):
                for tt in range(TT):
                    if CHOSEN_AT[tt] == u:
                        chosen_transposed(tt)
                if u < 2:
                    pe.wait_ge(pq_out, N_PQ)
                else:
                    pe.wait_ge(early_done, u - 1)
                block_scores(u % SL, U_DENSE + u + 1, u % 2)
            for tt in range(TT):
                if CHOSEN_AT[tt] == ROUTE_U:
                    chosen_transposed(tt)

            quads, share = P // QUAD, GATE_U * DC * QUAD // P

            def gates_of(i, first):
                for q in range(quads):
                    if not (first and q < 4):
                        pe.wait_ge(quad_out, quads * i + (q - 3))
                    batch = q * QUAD // HB
                    pe.wait_ge(hot_ready, P // HB * i + (batch + 1))
                    for k in range(QUAD):
                        tok = q * QUAD % HB + k
                        last = nc.tensor.matmul(psum[2 + q % 4][:, k * NK:(k + 1) * NK], hot[:, batch % 2, 0, tok, :],
                                                hot[:, batch % 2, 1, tok, :], start=True, stop=True)
                    last.then_inc(quad_done, 1)
                    u, c = q * share // DC, q * share % DC
                    if c == 0:
                        pe.wait_ge(early_done, GATE_U * i + (ROUTE_U + u - 1))
                    block_scores(u, U_GATE + GATE_U * i + (u + 1), u % 2, c, c + share)

            pe.wait_ge(chT_out, 3)
            gates_of(0, True)
            with pe.Fori(1, TT) as i:
                gates_of(i, False)

            def scores_of(first_slot, unit0, blocks_before):
                for j in range(GB):
                    if blocks_before is not None:
                        pe.wait_ge(w_done, blocks_before + (j + 1))
                    block_scores(first_slot + j, unit0 + (j + 1), j)

            def values_of(first_slot, unit0, parity, blocks, outs_before):
                pe.wait_ge(lo_done, unit0 + GB)
                pe.wait_ge(wsplit, blocks)
                for dc in range(DC):
                    if outs_before is not None or dc >= 4:
                        pe.wait_ge(o_out, (0 if outs_before is None else outs_before) + (dc - 3))
                    for j in range(GB):
                        last = three(psum[4 + dc % 4][:], wh[:, first_slot + j, dc * P:(dc + 1) * P],
                                     wl[:, first_slot + j, dc * P:(dc + 1) * P],
                                     act_h[:, parity, j, :], act_l[:, parity, j, :], j == 0, j == GB - 1)
                        if dc == DC - 1:
                            last.then_inc(unit_used, 1)
                    if dc < DC - 1:
                        last.then_inc(o_ready, 1)

            pe.wait_ge(quad_out, T // QUAD)
            pe.wait_ge(early_done, GB * EARLY)
            scores_of(U_S0 % SL, U_S0, None)
            values_of(U_V0 % SL, U_V0, 0, GB, None)
            values_of((U_V0 + GB) % SL, U_V0 + GB, 1, 2 * GB, DC)
            with pe.Fori(1, EARLY // 2) as i:
                for q in range(2):
                    values_of((U_V0 + GB * q) % SL, U_V0 + GB * q + 8 * i, q, GB * (1 + q) + 8 * i, DC * q + 16 * i)

            def turn_of(g, q, i):
                unit0 = U_SV + 2 * GB * (g + q - EARLY - 1)
                scores_of(U_SV % SL, unit0 + 16 * i, GB * (g + q - 1) + 8 * i)
                values_of((U_SV + GB) % SL, unit0 + GB + 16 * i, (g + q - 1) % 2, GB * (g + q) + 8 * i,
                          DC * (g + q - 1) + 16 * i)

            turn_of(EARLY + 1, 0, 0)
            with pe.Fori(0, (GROUPS - EARLY - 2) // 2) as i:
                for q in range(2):
                    turn_of(EARLY + 2, q, i)
            values_of((U_PLE - GB) % SL, U_PLE - GB, (GROUPS - 1) % 2, NK, DC * (GROUPS - 1))

            pe.wait_ge(w_done, NK)
            norm_sums(2, sq2)
            pe.wait_ge(pp_split, 4)
            pe.wait_ge(o_out, DC * GROUPS)
            for half in range(2):
                emb = U_PLE + 5 * half
                pe.wait_ge(lo_done, emb + 1)
                for k4 in range(4):
                    if half == 1:
                        pe.wait_ge(ple_out, k4 + 1)
                    for k in range(2):
                        last = three(psum[2 + k4][:], w(wh, emb, 2 * k4 + k), w(wl, emb, 2 * k4 + k),
                                     pt_h[:, k, :], pt_l[:, k, :], k == 0, k == 1)
                last.then_inc(unit_used, 1)
                for k4 in range(4):
                    dc = 4 * half + k4
                    if dc >= 2:
                        pe.wait_ge(ple_out, dc - 1)
                    project(emb + 1 + k4, dc % 2, h_from=2 * DC if dc == 0 else None)
            norm_sums(3, sq2)

        @block.scalar
        def _(act):
            for i in range(2):
                act.dma_start(x[:, 4 * i:4 * i + 4, :], xT[4 * i:4 * i + 4].rearrange("c p t -> p c t")).then_inc(x_in[i], 16)
            for dst, src in ((gain, gains), (wf, w_f), (bfb, b_f), (convw, conv_w)):
                act.dma_start(dst[:], src).then_inc(const_in, 16)

            def high(n, turn=None):
                act.wait_ge(raw_in[n % RAW], 16 * (n // RAW + 1) if turn is None else turn)
                nc.scalar.activation(wh[:, n % SL, :], raw[:, n % RAW, :], ACT.Copy).then_inc(hi_done, 1)

            def next_high(n, i=None):
                if i is None:
                    if n + SL < N_UNITS:
                        act.wait_ge(unit_used, n + 1)
                        high(n + SL)
                else:
                    step, i = i
                    act.wait_ge(unit_used, step * i + (n + 1))
                    high(n + SL, 16 * step // RAW * i + 16 * ((n + SL) // RAW + 1))

            def norm(k, sqb, hfb, x_sem, x_base, ahead=None):
                for c in range(DC):
                    if ahead is not None:
                        next_high(ahead + c)
                    if c >= 2:
                        act.wait_ge(sq_used, DC * k + c - 1)
                    if k == 0:
                        act.wait_ge(x_in[c // 4], 16)
                    else:
                        act.wait_ge(x_sem, x_base + c + 1)
                    nc.scalar.activation(sqb[:, c % 2, :], x[:, c, :], ACT.Square).then_inc(sq_ready, 1)
                act.wait_ge(var_ready, k + 1)
                nc.scalar.activation(rstd[:], rstd[:], ACT.Sqrt).then_inc(std_ready, 1)
                if k < 3:
                    for c in range(DC):
                        act.wait_ge(hf_ready, DC * k + c + 1)
                        nc.scalar.activation(hh[:, c, :], hfb[:, c % 2, :], ACT.Copy).then_inc(hh_ready, 1)

            norm(0, sq, hf, None, 0)
            for n in range(SL):
                high(n)
            act.wait_ge(unit_used, U_V + 4)
            for tt in range(TT):
                last = nc.scalar.activation(v_sb[:, tt, :], psum[tt][:], ACT.Copy)
            last.then_inc(v_out, 1)
            for n in range(4):
                next_high(U_V + n)
            act.wait_ge(f_abs, 1)
            nc.scalar.activation(fe[:], fa[:], ACT.Exp, scale=-1.0).then_inc(f_exp, 1)
            act.wait_ge(f_exp, 1)
            nc.scalar.activation(fa[:], fe[:], ACT.Ln, bias=ones[:, 0:1]).then_inc(f_ln, 1)

            def gate_rows(pair):
                if pair == 0:
                    act.wait_ge(cum_out, 2)
                if pair >= 2:
                    act.wait_ge(logits_ready, 2 * TT * (pair - 1))
                for e, (rq, rk) in enumerate(((HD, HD + 1), (0, 1))):
                    h = 2 * pair + e
                    act.dma_start(qa[rq:rq + 1, pair % 2, e, :], cum[h:h + 1, :]).then_inc(aug_in[pair % 2], 16)
                    act.dma_start(ka[rk:rk + 1, pair % 2, e, :], ncum[h:h + 1, :]).then_inc(aug_in[pair % 2], 16)

            def mix_out(m):
                act.wait_ge(unit_used, U_MIX + m + 1)
                kind = MIX[m]
                pair = (m + 2) // 5 if kind in "qk" else (m - 2) // 5
                if kind == "C":
                    if pair >= 1:
                        act.wait_ge(mix_dve, 2 * pair)
                    nc.scalar.activation(c_in, psum[m % 3][:], ACT.Copy).then_inc(mix_act, 1)
                    return
                dst = qa if kind == "q" else ka
                scale = HD ** -0.5 if kind == "q" else 1.0
                if m == 0:
                    act.wait_ge(rows_ready, 1)
                if pair >= 2:
                    act.wait_ge(logits_ready, 2 * TT * (pair - 1))
                for e in range(2):
                    r = slice(HD * e, HD * (e + 1))
                    last = nc.scalar.activation(dst[r, pair % 2, e, :], psum[m % 3][r, :], ACT.Copy, scale=scale)
                last.then_inc(mix_act, 1)

            mix_out(0)
            next_high(U_MIX)
            mix_out(1)
            next_high(U_MIX + 1)
            gate_rows(0)
            gate_rows(1)

            def probs_out(g):
                act.wait_ge(pT_ready, g + 1)
                if g >= 1:
                    act.wait_ge(pv_done, g)
                qi = g % TT
                nc.scalar.activation(probsT[:, 0:(qi + 1) * P], psum[5][:, 0:(qi + 1) * P], ACT.Copy).then_inc(pT_out, 1)

            m = 2
            for pair in range(PAIRS):
                units = 5 if pair < PAIRS - 1 else 3
                steps = units * DC
                for s in range(2 * TT):
                    for k in range(steps * s // (2 * TT), steps * (s + 1) // (2 * TT)):
                        mu = m + k // DC
                        if k % DC == DC - 1 and MIX[mu] in "qkC":
                            if MIX[mu] == "q" and pair >= 1:
                                gate_rows(pair + 1)
                            mix_out(mu)
                        if k % DC == DC - 1:
                            next_high(U_MIX + mu)
                    g = 2 * TT * pair + s
                    qi = s % TT
                    act.wait_ge(max_ready, g + 1)
                    if g >= 2:
                        act.wait_ge(pT_ready, g - 1)
                    nc.scalar.activation(probs[:, g % 2, 0:(qi + 1) * P], psum[3 + g % 2][:, 0:(qi + 1) * P], ACT.Exp,
                                         bias=nmax[:, g % 2:g % 2 + 1],
                                         accum_out=rsum[:, g % 2:g % 2 + 1]).then_inc(exp_done, 1)
                    if g >= 1:
                        probs_out(g - 1)
                m += units
            probs_out(2 * TT * PAIRS - 1)

            for dc in range(DC):
                b = 4 * (dc % 2)
                for k, buf in enumerate((sig_a, sig_c)):
                    act.wait_ge(unit_used, U_MERGE + 3 * dc + k + 1)
                    if dc >= 2:
                        act.wait_ge(mg_out, dc - 1)
                    elif dc == 0:
                        act.wait_ge(pv_done, 2 * TT * PAIRS)
                        act.wait_ge(mix_dve, by_dve(len(MIX)))
                    nc.scalar.activation(buf[:, dc % 2, :], psum[b + k][:], ACT.Sigmoid).then_inc(sig_done, 1)
                    next_high(U_MERGE + 3 * dc + k)
                next_high(U_MERGE + 3 * dc + 2)
            for c in range(DC):
                if c == 0:
                    act.wait_ge(unit_used, U_OUT)
                act.wait_ge(mg_out, c + 1)
                nc.scalar.activation(hh[:, c, :], merged[:, c, :], ACT.Copy).then_inc(mh_ready, 1)

            norm(1, sq1, hf1, wo_out, 0, ahead=U_OUT)
            act.dma_start(keys[:], keysT).then_inc(keys_in, 16)

            def score_out(n):
                act.wait_ge(sc_ready, n + 1)
                if n >= 2:
                    act.wait_ge(sc_used, n - 1)
                nc.scalar.activation(scores[:, n % 2], psum[2 + n % 2][:].rearrange("p (t n) -> p t n", t=TT),
                                     ACT.Copy).then_inc(sc_out, 1)

            for n in range(N_PQ):
                act.wait_ge(unit_used, U_PQ + n + 1)
                if n >= 2:
                    act.wait_ge(sc_ready, n - 1)
                nc.scalar.activation(qT[:, n % 2, :], psum[n % 2][:], ACT.Copy).then_inc(pq_out, 1)
                next_high(U_PQ + n)
                if n >= 1:
                    score_out(n - 1)
            score_out(N_PQ - 1)

            def early_gelu(par, used, before):
                act.wait_ge(unit_used, used)
                if before is not None:
                    act.wait_ge(gelu_out[par], before)
                nc.scalar.activation(gout[:, par, :], psum[par][:], ACT.Gelu).then_inc(early_done, 1)

            def store_gelu(par, done, block):
                act.wait_ge(early_done, done)
                act.dma_start(gelu_dram[block], gout[:, par, :]).then_inc(gelu_out[par], 16)

            for u in range(ROUTE_U):
                for tt in range(TT):
                    if EXP_AT[tt] == u:
                        act.wait_ge(top_ready, tt + 1)
                        nc.scalar.activation(top[:], top[:], ACT.Exp).then_inc(gexp, 1)
                early_gelu(u % 2, U_DENSE + u + 1, 16 * (u // 2) if u >= 2 else None)
                next_high(U_DENSE + u)
                store_gelu(u % 2, u + 1, u)

            quads = P // QUAD

            def gates_of(i, first):
                for q in range(quads):
                    chunk, k = divmod(q, GT // QUAD)
                    act.wait_ge(quad_done, quads * i + (q + 1))
                    if k == 0 and not (first and chunk < 2):
                        act.wait_ge(stage_out[chunk % 2], 32 * i + 16 * (chunk // 2))
                    nc.scalar.activation(stage[:, chunk % 2, :, QUAD * k:QUAD * (k + 1)].rearrange("p a t -> p t a"),
                                         psum[2 + q % 4][:].rearrange("p (t a) -> p t a", t=QUAD), ACT.Copy).then_inc(quad_out, 1)
                    if q % (quads // GATE_U) == quads // GATE_U - 1:
                        u = q // (quads // GATE_U)
                        early_gelu(u % 2, U_GATE + GATE_U * i + (u + 1),
                                   16 * (ROUTE_U // 2) + 16 * (GATE_U // 2) * i + 16 * (u // 2))
                        if first:
                            next_high(U_GATE + u)
                        else:
                            next_high(U_GATE + u, (GATE_U, i))
                        store_gelu(u % 2, GATE_U * i + (ROUTE_U + u + 1),
                                   ROUTE_U + u if first else bass.ds(GATE_U * i + (ROUTE_U + u), 1))
                    if k == GT // QUAD - 1:
                        act.wait_ge(quad_out, quads * i + (q + 1))
                        dst = gate_dram[chunk] if first else gate_dram[bass.ds((P // GT) * i + chunk, 1)].rearrange("o b a t -> (o b) a t")
                        act.dma_start(dst, stage[:, chunk % 2]).then_inc(stage_out[chunk % 2], 16)

            gates_of(0, True)
            with act.Fori(1, TT) as i:
                gates_of(i, False)
            for par in range(2):
                act.wait_ge(stage_out[par], 16 * (CH // 2))
                act.wait_ge(gelu_out[par], 16 * (GB * EARLY // 2))

            def load_gates(parity, blocks):
                act.dma_start(gate[:, parity], gate_dram[:, :, blocks, :].rearrange("c b a t -> b c a t")).then_inc(gate_in[parity], 16)

            def load_gelus(parity, blocks):
                act.dma_start(gelu_in[:, parity], gelu_dram[blocks].rearrange("a b t -> b a t")).then_inc(gelu_back[parity], 16)

            def gelus(unit0, i=None):
                for j in range(GB):
                    act.wait_ge(unit_used, unit0 + (j + 1) if i is None else 16 * i + (unit0 + (j + 1)))
                    nc.scalar.activation(psum[j][:], psum[j][:], ACT.Gelu).then_inc(gelu_done, 1)
                    next_high(unit0 + j, None if i is None else (16, i))

            def highs_after(unit0, i=None):
                for j in range(GB):
                    next_high(unit0 + j, None if i is None else (16, i))

            for g in range(2):
                load_gates(g, slice(GB * g, GB * g + GB))
                load_gelus(g, slice(GB * g, GB * g + GB))
            gelus(U_S0)
            with act.Fori(0, (EARLY - 2) // 2) as i:
                for q in range(2):
                    act.wait_ge(w_done, GB * (1 + q) + 8 * i)
                    load_gates(q, bass.ds(GB * (2 + q) + 8 * i, GB))
                    load_gelus(q, bass.ds(GB * (2 + q) + 8 * i, GB))
                    for j in range(GB):
                        next_high(U_V0 + GB * q + j, (8, i))
            for q in range(2):
                g = EARLY - 2 + q
                act.wait_ge(w_done, GB * (g + 1))
                load_gates(q, slice(GB * (g + 2), GB * (g + 3)))
                highs_after(U_V0 + GB * g)

            def turn_of(g, q, i):
                unit0 = U_SV + 2 * GB * (g + q - EARLY - 1)
                gelus(unit0, i)
                if i is None:
                    act.wait_ge(w_done, GB * g)
                    load_gates((g + 1) % 2, slice(GB * (g + 1), GB * (g + 2)))
                else:
                    act.wait_ge(w_done, GB * (g + q) + 8 * i)
                    load_gates((g + q + 1) % 2, bass.ds(GB * (g + q + 1) + 8 * i, GB))
                highs_after(unit0 + GB, i)

            turn_of(EARLY + 1, 0, None)
            with act.Fori(0, (GROUPS - EARLY - 2) // 2 - 1) as i:
                for q in range(2):
                    turn_of(EARLY + 2, q, i)
            for g in (GROUPS - 2, GROUPS - 1):
                unit0 = U_SV + 2 * GB * (g - EARLY - 1)
                gelus(unit0)
                if g == GROUPS - 2:
                    act.wait_ge(w_done, GB * g)
                    load_gates((g + 1) % 2, slice(GB * (g + 1), GB * (g + 2)))
                highs_after(unit0 + GB)
            highs_after(U_PLE - GB)

            act.wait_ge(w_done, NK)
            act.dma_start(pt[:], pT).then_inc(p_in, 16)
            norm(2, sq2, hf2, o_out, DC * (GROUPS - 1))
            next_high(U_PLE)
            next_high(U_PLE + 1)
            for dc in range(DC):
                act.wait_ge(unit_used, U_PLE + 5 * (dc // 4) + dc % 4 + 2)
                if dc >= 2:
                    act.wait_ge(ple_out, dc - 1)
                nc.scalar.activation(sg[:, dc % 2, :], psum[dc % 2][:], ACT.Sigmoid).then_inc(ple_sig, 1)
            norm(3, sq2, None, ple_out, 0)

        @block.vector
        def _(dve):
            chain = [0]

            def mark(ins):
                chain[0] += 1
                ins.then_inc(dve_own, 1)

            def link(ins):
                mark(ins)
                dve.wait_ge(dve_own, chain[0])

            def norm(k, hfb):
                dve.wait_ge(sq_used, DC * (k + 1))
                nc.vector.tensor_scalar(rstd[:], psum[NORM_BANK[k]][:], 1.0 / D, EPS, ALU.mult, ALU.add).then_inc(var_ready, 1)
                dve.wait_ge(std_ready, k + 1)
                link(nc.vector.reciprocal(rstd[:], rstd[:]))
                if k == 3:
                    for c in range(DC):
                        nc.vector.scalar_tensor_tensor(out=outb[:, c, :], in0=x[:, c, :], scalar=gain[:, k, c:c + 1],
                                                       in1=rstd[:], op0=ALU.mult, op1=ALU.mult).then_inc(out_ready, 1)
                    return
                for c in range(DC + 1):
                    if c < DC:
                        if c >= 2:
                            dve.wait_ge(h_ready, DC * k + c - 1)
                        nc.vector.scalar_tensor_tensor(out=hfb[:, c % 2, :], in0=x[:, c, :], scalar=gain[:, k, c:c + 1],
                                                       in1=rstd[:], op0=ALU.mult, op1=ALU.mult).then_inc(hf_ready, 1)
                    if c >= 1:
                        dve.wait_ge(hf_ready, DC * k + c)
                        dve.wait_ge(hh_ready, DC * k + c)
                        nc.vector.tensor_tensor(hl[:, c - 1, :], hfb[:, (c - 1) % 2, :], hh[:, c - 1, :].bitcast(F32),
                                                ALU.subtract).then_inc(h_ready, 1)

            link(nc.vector.memset(qa[0:HD, :, 1, :], 0.0))
            link(nc.vector.memset(ka[0:HD, :, 1, :], 0.0))
            nc.vector.memset(qa[0:2, :, 1, :], 1.0)
            nc.vector.memset(ka[0:2, :, 1, :], 1.0)
            nc.vector.memset(qa[HD:HD + 2, :, 0, :], 1.0)
            nc.vector.memset(z[:, 0:TAPS - 1], 0.0)
            link(nc.vector.memset(ka[HD:HD + 2, :, 0, :], 1.0))
            dve.wait_ge(const_in, 64)
            link(nc.vector.tensor_copy(wf_h[:], wf[:]))
            link(nc.vector.tensor_tensor(wf_l[:], wf[:], wf_h[:].bitcast(F32), ALU.subtract))
            nc.vector.memset(nmax[:], 0.0).then_inc(rows_ready, 1)
            norm(0, hf)

            dve.wait_ge(f_ready, 1)
            link(nc.vector.tensor_tensor(fz[:], psum[4][:, 0:TT * HEADS].rearrange("p (t h) -> p t h", t=TT),
                                         bfb[:].unsqueeze(1).to_broadcast([P, TT, HEADS]), ALU.add))
            link(nc.vector.tensor_scalar(fe[:], fz[:], -1.0, None, ALU.mult))
            nc.vector.tensor_tensor(fa[:], fz[:], fe[:], ALU.max).then_inc(f_abs, 1)
            link(nc.vector.tensor_scalar(fz[:], fz[:], 0.0, None, ALU.min))
            dve.wait_ge(f_ln, 1)
            nc.vector.tensor_tensor(logf[:], fz[:], fa[:], ALU.subtract).then_inc(logf_ready, 1)
            dve.wait_ge(cum_ready, 1)
            nc.vector.tensor_copy(cum[:], psum[5][0:HEADS, :]).then_inc(cum_out, 1)
            nc.vector.tensor_scalar(ncum[:], psum[5][0:HEADS, :], -1.0, None, ALU.mult).then_inc(cum_out, 1)

            def mix_out(m):
                kind, pair = MIX[m], (m - 2) // 5
                dve.wait_ge(unit_used, U_MIX + m + 1)
                if kind == "x":
                    dve.wait_ge(mix_act, by_act(m))
                    nc.vector.tensor_tensor(z[:, TAPS - 1:], psum[m % 3][:], c_in, ALU.mult).then_inc(mix_dve, 1)
                    dve.wait_ge(mix_dve, by_dve(m) + 1)
                    link(nc.vector.tensor_scalar(cv, z[:, 2:2 + T], convw[:, 2, pair:pair + 1], None, ALU.mult))
                    for tap in (1, 0):
                        link(nc.vector.scalar_tensor_tensor(out=cv, in0=z[:, tap:tap + T], scalar=convw[:, tap, pair:pair + 1],
                                                            in1=cv, op0=ALU.mult, op1=ALU.add))
                    return
                nc.vector.tensor_tensor(cv, psum[m % 3][:], cv, ALU.mult).then_inc(mix_dve, 1)
                dve.wait_ge(mix_dve, by_dve(m) + 1)
                link(nc.vector.tensor_copy(conv_h[:, pair, :], cv))
                link(nc.vector.tensor_tensor(conv_l[:, pair, :], cv, conv_h[:, pair, :].bitcast(F32), ALU.subtract))

            def pair_done(pair):
                dve.wait_ge(pv_done, 2 * TT * (pair + 1))
                bank = psum[6 + pair % 2]
                link(nc.vector.tensor_copy(attn_h[:, pair, :], bank[:]))
                nc.vector.tensor_tensor(attn_l[:, pair, :], bank[:], attn_h[:, pair, :].bitcast(F32),
                                        ALU.subtract).then_inc(pair_out, 1)

            m = 2
            for pair in range(PAIRS):
                units = 5 if pair < PAIRS - 1 else 3
                steps = units * DC
                for s in range(2 * TT):
                    for k in range(steps * s // (2 * TT), steps * (s + 1) // (2 * TT)):
                        mu = m + k // DC
                        if k % DC == DC - 1 and MIX[mu] in "xB":
                            mix_out(mu)
                    g = 2 * TT * pair + s
                    qi = s % TT
                    bank = psum[3 + g % 2]
                    diag = bank[:, qi * P:(qi + 1) * P]
                    dve.wait_ge(logits_ready, g + 1)
                    link(nc.vector.tensor_tensor(diag, diag, mask[:], ALU.add))
                    nc.vector.tensor_reduce(nmax[:, g % 2:g % 2 + 1], bank[:, 0:(qi + 1) * P], AX.X, ALU.max,
                                            negate=True).then_inc(max_ready, 1)
                    dve.wait_ge(exp_done, g + 1)
                    link(nc.vector.reciprocal(rsum[:, g % 2:g % 2 + 1], rsum[:, g % 2:g % 2 + 1]))
                    row = probs[:, g % 2, 0:(qi + 1) * P]
                    nc.vector.tensor_scalar(row, row, rsum[:, g % 2:g % 2 + 1], None, ALU.mult).then_inc(probs_ready, 1)
                    if pair >= 1 and s == 2:
                        pair_done(pair - 1)
                m += units
            pair_done(PAIRS - 1)

            for dc in range(DC):
                b = 4 * (dc % 2)
                dve.wait_ge(unit_used, U_MERGE + 3 * dc + 3)
                dve.wait_ge(sig_done, 2 * dc + 2)
                mark(nc.vector.tensor_tensor(sig_a[:, dc % 2, :], psum[b + 2][:], sig_a[:, dc % 2, :], ALU.mult))
                link(nc.vector.tensor_tensor(sig_c[:, dc % 2, :], psum[b + 3][:], sig_c[:, dc % 2, :], ALU.mult))
                nc.vector.tensor_tensor(merged[:, dc, :], sig_a[:, dc % 2, :], sig_c[:, dc % 2, :], ALU.add).then_inc(mg_out, 1)
            for c in range(DC):
                dve.wait_ge(mg_out, c + 1)
                dve.wait_ge(mh_ready, c + 1)
                nc.vector.tensor_tensor(hl[:, c, :], merged[:, c, :], hh[:, c, :].bitcast(F32), ALU.subtract).then_inc(ml_ready, 1)
            for dc in range(DC):
                dve.wait_ge(unit_used, U_OUT + dc + 1)
                nc.vector.tensor_tensor(x[:, dc, :], psum[dc % 4][:], x[:, dc, :], ALU.add).then_inc(wo_out, 1)
            norm(1, hf1)

            def best(rows):
                own = [0] * len(rows)
                for step in range(5):
                    for k, (values, vals, idx) in enumerate(rows):
                        if step:
                            dve.wait_ge(dve_own, own[k])
                        half = slice(0, 8) if step < 3 else slice(8, 16)
                        if step in (0, 3):
                            mark(nc.vector.max(vals[:, half], values))
                        elif step in (1, 4):
                            mark(nc.vector.max_index(idx[:, half], vals[:, half], values))
                        else:
                            mark(nc.vector.match_replace(values, vals[:, half], values, MASKED))
                        own[k] = chain[0]

            for n in range(N_PQ):
                dve.wait_ge(sc_out, n + 1)
                best([(scores[:, n % 2, tt, :], v12[:, tt, n, :], i12[:, tt, n, :]) for tt in range(TT)])
                dve.wait_ge(dve_own, chain[0])
                nc.vector.memset(gsum[:, 0, 0:1], 0.0).then_inc(sc_used, 1)

            for tt in range(TT):
                vv = v12[:, tt].rearrange("p (h s) k -> p h s k", s=2)
                link(nc.vector.tensor_tensor(cand[:], vv[:, :, 0, :].unsqueeze(3).to_broadcast([P, PH, TOPK, TOPK]),
                                             vv[:, :, 1, :].unsqueeze(2).to_broadcast([P, PH, TOPK, TOPK]), ALU.add))
                best([(cand[:, h, :, :].rearrange("p a b -> p (a b)"), top[:, h, :], topj[:, h, :]) for h in range(PH)])
                dve.wait_ge(dve_own, chain[0])
                link(nc.vector.tensor_copy(gsum[:, 1, :], top[:, :, 0]))
                nc.vector.tensor_tensor(top[:], top[:], gsum[:, 1, :].unsqueeze(2).to_broadcast([P, PH, TOPK]),
                                        ALU.subtract).then_inc(top_ready, 1)
                tj = topj[:].rearrange("p h k -> p (h k)")
                mark(nc.vector.tensor_scalar(rank[:, 0, :], tj, 4, None, ALU.logical_shift_right))
                mark(nc.vector.tensor_scalar(rank[:, 1, :], tj, TOPK - 1, None, ALU.bitwise_and))
                mark(nc.vector.tensor_copy(i12b[:], i12[:, tt]))
                dve.wait_ge(dve_own, chain[0] - 1)
                link(nc.vector.tensor_copy(rankb[:], rank[:]))
                ii = i12b[:].rearrange("p (h s) k -> p h s k", s=2)
                for side in range(2):
                    if side == 0 and tt >= 2:
                        dve.wait_ge(chT_ready, 3 * (tt - 1))
                    elif side == 1:
                        dve.wait_ge(chosen_ready, 3 * tt + 1)
                    link(nc.vector.tensor_tensor(onehot[:], rankb[:, side, :].unsqueeze(2).to_broadcast([P, HK, TOPK]),
                                                 iota_k[:].unsqueeze(1).to_broadcast([P, HK, TOPK]), ALU.is_equal))
                    hot4 = onehot[:].rearrange("p (h k) r -> p h k r", h=PH)
                    link(nc.vector.tensor_tensor(hot4, hot4, ii[:, :, side, :].unsqueeze(2).to_broadcast([P, PH, TOPK, TOPK]),
                                                 ALU.mult))
                    nc.vector.tensor_reduce(chosen[:, tt % 2, side, :], onehot[:], AX.X, ALU.add).then_inc(chosen_ready, 1)
                dve.wait_ge(gexp, tt + 1)
                link(nc.vector.tensor_reduce(gsum[:, 0, :], top[:], AX.X, ALU.add))
                link(nc.vector.reciprocal(gsum[:, 0, :], gsum[:, 0, :]))
                nc.vector.tensor_tensor(chosen[:, tt % 2, 2, :].rearrange("p (h k) -> p h k", h=PH), top[:],
                                        gsum[:, 0, :].unsqueeze(2).to_broadcast([P, PH, TOPK]),
                                        ALU.mult).then_inc(chosen_ready, 1)
            dve.wait_ge(chT_ready, 3 * TT)
            nc.vector.tensor_copy(i1T[:], psum[4][:]).then_inc(chT_out, 1)
            nc.vector.tensor_copy(i2T[:], psum[5][:]).then_inc(chT_out, 1)
            nc.vector.tensor_copy(gT[:], psum[6][:]).then_inc(chT_out, 1)
            dve.wait_ge(chT_out, 3)

            def one_hots(buf, batch, first):
                if not first:
                    dve.wait_ge(quad_done, HB // QUAD * batch - HB // QUAD)
                at = slice(HB * batch, HB * batch + HB) if first else bass.ds(HB * batch, HB)
                keys_b = iota_nk[:].unsqueeze(1).to_broadcast([P, HB, NK])
                nc.vector.tensor_tensor(hot[:, buf, 1], keys_b, i1T[:, at].unsqueeze(2).to_broadcast([P, HB, NK]),
                                        ALU.is_equal).then_inc(hot_own, 1)
                nc.vector.tensor_tensor(hot[:, buf, 0], keys_b, i2T[:, at].unsqueeze(2).to_broadcast([P, HB, NK]), ALU.is_equal)
                dve.wait_ge(hot_own, batch + 1)
                nc.vector.tensor_tensor(hot[:, buf, 1], hot[:, buf, 1], gT[:, at].unsqueeze(2).to_broadcast([P, HB, NK]),
                                        ALU.mult).then_inc(hot_ready, 1)

            for k in range(2):
                one_hots(k, k, True)
            with dve.Fori(1, T // HB // 2) as i:
                for k in range(2):
                    one_hots(k, 2 * i + k, False)

            def weigh(parity, blocks, gate_turn, early_turn, buffer_free):
                for j in range(GB):
                    if early_turn is None:
                        dve.wait_ge(gelu_done, blocks + (j + 1 - GB * EARLY))
                        gelu = psum[j][:]
                    else:
                        gelu = gelu_in[:, parity, j, :]
                    if j == 0:
                        dve.wait_ge(gate_in[parity], gate_turn)
                        if early_turn is not None:
                            dve.wait_ge(gelu_back[parity], early_turn)
                        if buffer_free is not None:
                            dve.wait_ge(unit_used, buffer_free)
                    nc.vector.tensor_tensor(wt[:, j % 2, :].rearrange("p (c t) -> p c t", c=CH),
                                            gelu.rearrange("p (c t) -> p c t", c=CH), gate[:, parity, :, j, :],
                                            ALU.mult).then_inc(w_done, 1)
                    dve.wait_ge(w_done, blocks + (j + 1))
                    nc.vector.tensor_copy(act_h[:, parity, j, :], wt[:, j % 2, :]).then_inc(wcopy, 1)
                    dve.wait_ge(wcopy, blocks + (j + 1))
                    nc.vector.tensor_tensor(act_l[:, parity, j, :], wt[:, j % 2, :], act_h[:, parity, j, :].bitcast(F32),
                                            ALU.subtract).then_inc(wsplit, 1)

            def add_values(outs, unit0):
                for dc in range(DC):
                    if dc < DC - 1:
                        dve.wait_ge(o_ready, outs + (dc + 1))
                    else:
                        dve.wait_ge(unit_used, unit0 + GB)
                    nc.vector.tensor_tensor(x[:, dc, :], psum[4 + dc % 4][:], x[:, dc, :], ALU.add).then_inc(o_out, 1)

            SENT = DC - 1
            weigh(0, 0, 16, 16, None)
            weigh(1, GB, 16, 16, None)
            add_values(0, U_V0)
            with dve.Fori(0, (EARLY - 2) // 2) as i:
                for q in range(2):
                    g = 1 + q
                    weigh((g + 1) % 2, GB * (g + 1) + 8 * i, 16 * i + 32, 16 * i + 32, 8 * i + (U_V0 + GB * g))
                    add_values(SENT * g + 2 * SENT * i, U_V0 + GB * g + 8 * i)
            g = EARLY - 1
            weigh(0, GB * EARLY, 16 * (EARLY // 2 + 1), None, U_V0 + GB * g)
            add_values(SENT * g, U_V0 + GB * g)

            def turn_of(g, q, i):
                unit0 = U_SV + 2 * GB * (g + q - EARLY - 1)
                weigh((g + q) % 2, GB * (g + q) + 8 * i, 16 * ((g + q) // 2 + 1) + 16 * i, None, None)
                add_values(SENT * (g + q - 1) + 2 * SENT * i, unit0 + GB + 16 * i)

            turn_of(EARLY + 1, 0, 0)
            with dve.Fori(0, (GROUPS - EARLY - 2) // 2) as i:
                for q in range(2):
                    turn_of(EARLY + 2, q, i)
            add_values(SENT * (GROUPS - 1), U_PLE - GB)

            dve.wait_ge(p_in, 16)
            for k in range(2):
                nc.vector.tensor_copy(pt_h[:, k, :], pt[:, k, :]).then_inc(pp_split, 1)
                dve.wait_ge(pp_split, 2 * k + 1)
                nc.vector.tensor_tensor(pt_l[:, k, :], pt[:, k, :], pt_h[:, k, :].bitcast(F32), ALU.subtract).then_inc(pp_split, 1)
            norm(2, hf2)
            for dc in range(DC):
                dve.wait_ge(ple_sig, dc + 1)
                link(nc.vector.tensor_tensor(upd[:, dc % 2, :], psum[2 + dc % 4][:], sg[:, dc % 2, :], ALU.mult))
                nc.vector.tensor_tensor(x[:, dc, :], x[:, dc, :], upd[:, dc % 2, :], ALU.add).then_inc(ple_out, 1)
            norm(3, None)


def weight_stream(np, w_in, w_branch, w_out, w_peer_q, peer_u, peer_v, w_ple_gate, w_ple_proj):
    def tiles(w):
        k, n = w.shape
        return w.reshape(k // P, P, n // P, P).transpose(2, 1, 0, 3).reshape(n // P, P, -1)

    q, k, v, _, B, C, xc, ga, gc = np.split(w_in, np.cumsum([CW, CW, CW, HEADS, CW, CW, CW, D]), axis=1)
    vt = v.reshape(4, 2, P, CW).transpose(0, 2, 1, 3).reshape(4, P, UW)
    parts = {n: tiles(a) for n, a in (("q", q), ("k", k), ("C", C), ("x", xc), ("B", B))}
    at = dict.fromkeys(parts, 0)
    units = list(vt)
    for kind in MIX:
        units.append(parts[kind][at[kind]])
        at[kind] += 1
    ga, gc = tiles(ga), tiles(gc)
    branches = np.concatenate([tiles(w_branch[0]), tiles(w_branch[1])], axis=2)
    for dc in range(DC):
        units += [ga[dc], gc[dc], branches[dc]]
    units += list(tiles(w_out))
    units += list(tiles(w_peer_q.reshape(D, N_PQ * P)))
    u = peer_u.reshape(NK, NK, DC, P).transpose(0, 3, 2, 1).reshape(NK, P, UW)
    v = peer_v.reshape(NK, NK, D)
    group = [slice(GB * g, GB * g + GB) for g in range(GROUPS)]
    units += list(u[:GB * (EARLY + 1)])
    units += list(v[:GB * EARLY])
    for g in range(EARLY + 1, GROUPS):
        units += list(u[group[g]]) + list(v[group[g - 1]])
    units += list(v[group[-1]])
    gate = tiles(w_ple_gate)
    emb = w_ple_proj.reshape(2, P, 2, 4, P).transpose(2, 1, 3, 0, 4).reshape(2, P, UW)
    for half in range(2):
        units += [emb[half]] + list(gate[4 * half:4 * half + 4])
    return np.stack(units)


def kernel(**inputs):
    import numpy as np
    import concourse.bacc as bacc
    from concourse.bass_utils import run_bass_kernel_spmd

    a = {n: np.asarray(v) for n, v in inputs.items()}
    w_in = a["w_in"][0]
    arrays = {
        "xT": a["x"][0].T.reshape(DC, P, T),
        "pT": a["p"][0, 0].T.reshape(2, P, T).transpose(1, 0, 2),
        "stream": weight_stream(np, w_in, a["w_branch"][0], a["w_out"][0], a["w_peer_q"][0], a["peer_u"][0],
                                a["peer_v"][0], a["w_ple_gate"][0], a["w_ple_proj"][0]),
        "w_f": w_in[:, 3 * CW:3 * CW + HEADS].reshape(DC, P, HEADS).transpose(1, 0, 2),
        "b_f": np.broadcast_to(a["b_f"][0], (P, HEADS)),
        "conv_w": a["conv_w"][0].reshape(TAPS, CC, P).transpose(2, 0, 1),
        "gains": np.stack([a["g_mix"][0], a["g_ffn"][0], a["g_ple"][0], a["g_final"]]).reshape(4, DC, P).transpose(2, 0, 1),
        "keysT": np.stack([a["peer_k1"][0], a["peer_k2"][0]], axis=1).reshape(N_PQ, NK, P).transpose(2, 0, 1),
    }
    arrays = {n: np.ascontiguousarray(v) for n, v in arrays.items()}
    nc = bacc.Bacc("TRN2", target_bir_lowering=False, num_devices=1)
    args = {n: nc.dram_tensor(n, v.shape, mybir.dt.from_np(v.dtype), kind="ExternalInput").ap() for n, v in arrays.items()}
    gate_dram = nc.dram_tensor("gate_dram", (CH, P, NK, GT), F32, kind="Internal").ap()
    gelu_dram = nc.dram_tensor("gelu_dram", (GB * EARLY, P, T), F32, kind="Internal").ap()
    outT = nc.dram_tensor("outT", (DC, P, T), F32, kind="ExternalOutput").ap()
    peer_block_kernel(nc, gate_dram=gate_dram, gelu_dram=gelu_dram, outT=outT, **args)
    r = run_bass_kernel_spmd(nc, [arrays], core_ids=[0])
    return r.results[0]["outT"].reshape(D, T).T.reshape(1, T, D)
```

```python
from contextlib import ExitStack

import concourse.bass as bass
from concourse import mybir

F32 = mybir.dt.float32
F32R = mybir.dt.float32r
BF16 = mybir.dt.bfloat16
U32 = mybir.dt.uint32
ALU = mybir.AluOpType
ACT = mybir.ActivationFunctionType
AX = mybir.AxisListType

P = 128
T = 512
TT = T // P
D = 1024
DC = D // P
HEADS = 8
PAIRS = HEADS // 2
HD = 64
CW = 512
CC = CW // P
TAPS = 3
PH = 8
NK = 128
TOPK = 16
HK = PH * TOPK
CAND = TOPK * TOPK
PLE = 256
EPS = 1e-6
MASKED = -3.0e38

UW = 1024
U_V = 0
U_MIX = U_V + 4
N_MIX = 5 * PAIRS
U_MERGE = U_MIX + N_MIX
N_MERGE = 3 * DC
U_OUT = U_MERGE + N_MERGE
U_PQ = U_OUT + DC
N_PQ = 2 * PH
U_DENSE = U_PQ + N_PQ
GB = 4
GROUPS = NK // GB
ROUTE_U = 32
GATE_U = 16
EARLY = (ROUTE_U + GATE_U * TT) // GB
U_GATE = U_DENSE + ROUTE_U
U_S0 = U_GATE + GATE_U * TT
U_V0 = U_S0 + GB
U_SV = U_V0 + GB * EARLY
U_PLE = U_DENSE + 2 * NK
N_UNITS = U_PLE + DC + 2
RAW = 4
SL = 8

MIX = ["q", "k"]
for _i in range(PAIRS):
    MIX += ["C", "x"] + (["q", "k"] if _i < PAIRS - 1 else []) + ["B"]
PAIR_CHUNKS = [36, 36, 40, 32]


def pair_share(pair, s):
    start, n = sum(PAIR_CHUNKS[:pair]), PAIR_CHUNKS[pair]
    return range(start + n * s // (2 * TT), start + n * (s + 1) // (2 * TT))

GT = 32
CH = T // GT
HB = 8
QUAD = 4
EXP_AT = (7, 13, 18, 23)
CHOSEN_AT = (9, 15, 21, 28)


def peer_block_kernel(nc, xT, pT, stream, w_f, b_f, conv_w, gains, keysT, gate_dram, gelu_dram, outT):
    ctx = ExitStack()
    with ctx:
        def sb(name, shape, dt, where=ctx):
            return where.enter_context(nc.sbuf_tensor(name, shape, dt))

        def sem(name):
            return ctx.enter_context(nc.semaphore(name))

        x = sb("x", [P, DC, T], F32)
        hh = sb("hh", [P, DC, T], F32R)
        hl = sb("hl", [P, DC, T], F32R)
        raw = sb("raw", [P, RAW, UW], F32)
        wh = sb("wh", [P, SL, UW], F32R)
        wl = sb("wl", [P, SL, UW], F32R)
        ones = sb("ones", [P, P], F32)
        mean_w = sb("mean_w", [P, 1], F32)
        eps = sb("eps", [P, 1], F32)
        factor = sb("factor", [P, TT], F32)
        ident = sb("ident", [P, P], F32)
        iota_nk = sb("iota_nk", [P, NK], F32)
        iota_k = sb("iota_k", [P, TOPK], BF16)
        gain = sb("gain", [P, 4, DC], F32)
        rstd = sb("rstd", [P, T], F32)

        mix = ExitStack()
        sq = sb("sq", [P, 2, T], F32, mix)
        hf = sb("hf", [P, 2, T], F32, mix)
        attn_h = sb("attn_h", [P, CC, T], F32R, mix)
        attn_l = sb("attn_l", [P, CC, T], F32R, mix)
        conv_h = sb("conv_h", [P, CC, T], F32R, mix)
        conv_l = sb("conv_l", [P, CC, T], F32R, mix)
        att = ExitStack()
        v_sb = sb("v_sb", [P, TT, CW], F32, att)
        qa = sb("qa", [P, 2, 2, T], F32, att)
        ka = sb("ka", [P, 2, 2, T], F32, att)
        probs = [sq[:, 0, :], sq[:, 1, :], rstd[:]]
        probsT = sb("probsT", [P, T], F32, att)
        c_in = hf[:, 1, :]
        cv = hf[:, 0, :]
        z = sb("z", [P, T + TAPS - 1], F32, att)
        tri = sb("tri", [P, T], F32, att)
        mask = sb("mask", [P, P], F32, att)
        wf = sb("wf", [P, DC, HEADS], F32, att)
        wf_h = sb("wf_h", [P, DC, HEADS], F32R, att)
        wf_l = sb("wf_l", [P, DC, HEADS], F32R, att)
        bfb = sb("bfb", [P, HEADS], F32, att)
        fz = sb("fz", [P, TT, HEADS], F32, att)
        fa = sb("fa", [P, TT, HEADS], F32, att)
        fe = sb("fe", [P, TT, HEADS], F32, att)
        logf = sb("logf", [P, TT, HEADS], F32, att)
        cum = sb("cum", [HEADS, T], F32, att)
        ncum = sb("ncum", [HEADS, T], F32, att)
        convw = sb("convw", [P, TAPS, CC], F32, att)
        nmax = sb("nmax", [P, 3], F32, att)
        rsum = sb("rsum", [P, 3], F32, att)
        att.close()
        mrg = ExitStack()
        merged = sb("merged", [P, DC, T], F32, mrg)
        sig_a = sb("sig_a", [P, 2, T], F32, mrg)
        sig_c = sb("sig_c", [P, 2, T], F32, mrg)
        mrg.close()
        mix.close()
        rt = ExitStack()
        gout = sb("gout", [P, 4, T], F32, rt)
        sq1 = gout[:, 0:2, :]
        hf1 = gout[:, 2:4, :]
        i1T = sb("i1T", [P, T], F32, rt)
        i2T = sb("i2T", [P, T], F32, rt)
        gT = sb("gT", [P, T], F32, rt)
        gT_h = sb("gT_h", [P, T], F32R, rt)
        gT_l = sb("gT_l", [P, T], F32R, rt)
        rs = ExitStack()
        keys = sb("keys", [P, N_PQ, NK], F32, rs)
        qT = hf1
        scores = sb("scores", [P, 2, TT, NK], F32, rs)
        cand = sb("cand", [P, PH, TOPK, TOPK], F32, rs)
        v12 = sb("v12", [P, TT, N_PQ, TOPK], F32, rs)
        i12 = sb("i12", [P, TT, N_PQ, TOPK], U32, rs)
        i12b = sb("i12b", [P, N_PQ, TOPK], BF16, rs)
        top = sb("top", [P, PH, TOPK], F32, rs)
        topj = sb("topj", [P, PH, TOPK], U32, rs)
        rank = sb("rank", [P, 2, HK], U32, rs)
        rankb = sb("rankb", [P, 2, HK], BF16, rs)
        onehot = sb("onehot", [P, HK, TOPK], BF16, rs)
        gsum = sb("gsum", [P, 2, PH], F32, rs)
        chosen = sb("chosen", [P, 2, 3, HK], F32, rs)
        rs.close()
        gs = ExitStack()
        hot = sb("hot", [P, 2, 3, HB, NK], F32R, gs)
        stage = sb("stage", [P, 2, NK, GT], F32, gs)
        gs.close()
        rt.close()
        ex = ExitStack()
        gate = sb("gate", [P, 2, CH, GB, GT], F32, ex)
        gelu_in = sb("gelu_in", [P, 2, GB, T], F32, ex)
        wt = sb("wt", [P, 2, T], F32, ex)
        act_h = sb("act_h", [P, 2, GB, T], F32R, ex)
        act_l = sb("act_l", [P, 2, GB, T], F32R, ex)
        ex.close()
        pl = ExitStack()
        sq2 = sb("sq2", [P, 2, T], F32, pl)
        hf2 = sb("hf2", [P, 2, T], F32, pl)
        pt = sb("pt", [P, 2, T], F32, pl)
        pt_h = sb("pt_h", [P, 2, T], F32R, pl)
        pt_l = sb("pt_l", [P, 2, T], F32R, pl)
        sg = sb("sg", [P, 2, T], F32, pl)
        upd = sb("upd", [P, 2, T], F32, pl)
        outb = sb("outb", [P, DC, T], F32, pl)
        pl.close()
        psum = [ctx.enter_context(nc.psum_tensor(f"bank{b}", [P, T], F32)) for b in range(8)]

        x_in = [sem(f"x_in{i}") for i in range(4)]
        const_in = sem("const_in")
        keys_in = sem("keys_in")
        p_in = sem("p_in")
        raw_in = [sem(f"raw_in{i}") for i in range(RAW)]
        hi_done = sem("hi_done")
        lo_done = sem("lo_done")
        unit_used = sem("unit_used")
        consts = sem("consts")
        consts2 = sem("consts2")
        sq_ready = sem("sq_ready")
        sq_used = sem("sq_used")
        sum_ready = sem("sum_ready")
        std_ready = sem("std_ready")
        diag_ready = sem("diag_ready")
        row_ready = sem("row_ready")
        hf_ready = sem("hf_ready")
        hh_ready = sem("hh_ready")
        h_ready = sem("h_ready")
        v_out = sem("v_out")
        f_ready = sem("f_ready")
        f_abs = sem("f_abs")
        f_exp = sem("f_exp")
        f_ln = sem("f_ln")
        logf_ready = sem("logf_ready")
        cum_ready = sem("cum_ready")
        cum_out = sem("cum_out")
        aug_in = [sem(f"aug_in{i}") for i in range(2)]
        mix_act = sem("mix_act")
        mix_dve = sem("mix_dve")
        logits_ready = sem("logits_ready")
        max_ready = sem("max_ready")
        exp_done = sem("exp_done")
        probs_ready = sem("probs_ready")
        pT_ready = sem("pT_ready")
        pT_out = sem("pT_out")
        pv_done = sem("pv_done")
        pair_out = sem("pair_out")
        sig_done = sem("sig_done")
        mg_out = sem("mg_out")
        mh_ready = sem("mh_ready")
        ml_ready = sem("ml_ready")
        wo_out = sem("wo_out")
        pq_out = sem("pq_out")
        sc_ready = sem("sc_ready")
        sc_out = sem("sc_out")
        top_ready = sem("top_ready")
        gexp = sem("gexp")
        chosen_ready = sem("chosen_ready")
        chT_ready = sem("chT_ready")
        chT_out = sem("chT_out")
        hot_ready = sem("hot_ready")
        sc_used = sem("sc_used")
        hot_own = sem("hot_own")
        quad_done = sem("quad_done")
        quad_out = sem("quad_out")
        stage_out = [sem(f"stage_out{i}") for i in range(2)]
        gelu_out = [sem(f"gelu_out{i}") for i in range(4)]
        early_done = sem("early_done")
        gelu_back = [sem(f"gelu_back{i}") for i in range(2)]
        gate_in = [sem(f"gate_in{i}") for i in range(2)]
        gelu_done = sem("gelu_done")
        wcopy = sem("wcopy")
        rows_ready = sem("rows_ready")
        wf_split = sem("wf_split")
        w_done = sem("w_done")
        wsplit = sem("wsplit")
        o_ready = sem("o_ready")
        o_out = sem("o_out")
        pp_split = sem("pp_split")
        ple_sig = sem("ple_sig")
        ple_out = sem("ple_out")
        out_ready = sem("out_ready")
        stored = sem("stored")
        dve_own = sem("dve_own")

        block = ctx.enter_context(nc.Block())

        def by_act(m):
            return sum(k in "qkC" for k in MIX[:m])

        def by_dve(m):
            return sum(k in "xB" for k in MIX[:m])

        def wait_mix_out(eng, m):
            if MIX[m] in "qkC":
                eng.wait_ge(mix_act, by_act(m) + 1)
            else:
                eng.wait_ge(mix_dve, by_dve(m) + 1)

        @block.sync
        def _(sp):
            for i in range(4):
                sp.dma_start(x[:, 2 * i:2 * i + 2, :], xT[2 * i:2 * i + 2].rearrange("c p t -> p c t")).then_inc(x_in[i], 16)
            for n in range(SL):
                if n >= RAW:
                    sp.wait_ge(lo_done, n - RAW + 1)
                sp.dma_start(raw[:, n % RAW, :], stream[n]).then_inc(raw_in[n % RAW], 16)
            with sp.Fori(1, N_UNITS // SL) as i:
                for u in range(SL):
                    sp.wait_ge(lo_done, SL * i + (u - RAW + 1))
                    sp.dma_start(raw[:, u % RAW, :],
                                 stream[bass.ds(SL * i + u, 1)].rearrange("o p w -> p (o w)")).then_inc(raw_in[u % RAW], 16)
            for n in range(N_UNITS // SL * SL, N_UNITS):
                sp.wait_ge(lo_done, n - RAW + 1)
                sp.dma_start(raw[:, n % RAW, :], stream[n]).then_inc(raw_in[n % RAW], 16)

            for c in range(DC):
                sp.wait_ge(out_ready, c + 1)
                sp.dma_start(outT[c], outb[:, c, :]).then_inc(stored, 16)
            sp.wait_ge(stored, 16 * DC)

        @block.gpsimd
        def _(pool):
            nc.gpsimd.memset(mean_w[:], 1.0 / D).then_inc(consts, 1)
            nc.gpsimd.memset(ones[:], 1.0).then_inc(consts, 1)
            nc.gpsimd.memset(eps[:], EPS).then_inc(consts, 1)
            nc.gpsimd.memset(ident[:], 0.0).then_inc(consts, 1)
            nc.gpsimd.memset(tri[:], 1.0).then_inc(consts, 1)
            nc.gpsimd.memset(mask[:], 0.0).then_inc(consts, 1)
            pool.wait_ge(consts, 6)
            nc.gpsimd.affine_select(out=ident[:], in_=ident[:], compare_op=ALU.not_equal, fill=1.0, base=0,
                                    pattern=[[-1, P]], channel_multiplier=1).then_inc(consts2, 1)
            nc.gpsimd.affine_select(out=tri[:], in_=tri[:], compare_op=ALU.is_ge, fill=0.0, base=0,
                                    pattern=[[1, T]], channel_multiplier=-1).then_inc(consts2, 1)
            nc.gpsimd.affine_select(out=mask[:], in_=mask[:], compare_op=ALU.is_ge, fill=MASKED, base=0,
                                    pattern=[[-1, P]], channel_multiplier=1).then_inc(consts2, 1)
            nc.gpsimd.iota(iota_nk[:], pattern=[[1, NK]], base=0, channel_multiplier=0,
                           allow_small_or_imprecise_dtypes=True).then_inc(consts2, 1)
            nc.gpsimd.iota(iota_k[:], pattern=[[1, TOPK]], base=0, channel_multiplier=0,
                           allow_small_or_imprecise_dtypes=True).then_inc(consts2, 1)

            def low(u, unit):
                pool.wait_ge(hi_done, unit + 1)
                nc.gpsimd.tensor_tensor(wl[:, u, :], raw[:, u % RAW, :], wh[:, u, :].bitcast(F32),
                                        ALU.subtract).then_inc(lo_done, 1)

            for u in range(SL):
                low(u, u)
            with pool.Fori(1, N_UNITS // SL) as i:
                for u in range(SL):
                    low(u, SL * i + u)
            for n in range(N_UNITS // SL * SL, N_UNITS):
                low(n % SL, n)

        @block.tensor
        def _(pe):
            def three(out, ah, al, bh, bl, start, stop):
                nc.tensor.matmul(out, ah, bh, start=start, stop=False)
                nc.tensor.matmul(out, ah, bl, start=False, stop=False)
                return nc.tensor.matmul(out, al, bh, start=False, stop=stop)

            def w(part, n, c):
                return part[:, n % SL, c * P:(c + 1) * P]

            def project(n, bank, c0=0, c1=DC):
                for c in range(c0, c1):
                    if c == 0:
                        pe.wait_ge(lo_done, n + 1)
                    last = three(psum[bank][:], w(wh, n, c), w(wl, n, c), hh[:, c, :], hl[:, c, :], c == 0, c == DC - 1)
                if c1 == DC:
                    last.then_inc(unit_used, 1)
                return last

            def project_pair(n, bank, chunks_ready, before):
                pe.wait_ge(lo_done, n + 2)
                for c in range(DC):
                    pe.wait_ge(chunks_ready, before + c + 1)
                    for k in range(2):
                        last = three(psum[bank + k][:], w(wh, n + k, c), w(wl, n + k, c), hh[:, c, :], hl[:, c, :],
                                     c == 0, c == DC - 1)
                        if c == DC - 1:
                            last.then_inc(unit_used, 1)

            def norm_sums(k):
                pe.wait_ge(sq_used, DC * (k + 1))
                for tt in range(TT):
                    last = nc.tensor.matmul(psum[6][:, tt:tt + 1], rstd[:, tt * P:(tt + 1) * P], mean_w[:], start=True, stop=True)
                last.then_inc(sum_ready, 1)
                for tt in range(TT):
                    cols = slice(tt * P, (tt + 1) * P)
                    pe.wait_ge(diag_ready, TT * k + tt + 1)
                    last = nc.tensor.matmul(psum[7][:, cols], ones[:], rstd[:, cols], start=True, stop=True)
                last.then_inc(row_ready, 1)

            pe.wait_ge(consts2, 5)
            norm_sums(0)
            pe.wait_ge(wf_split, 1)
            for j in range(4):
                pe.wait_ge(lo_done, U_V + j + 1)
                for c in (2 * j, 2 * j + 1):
                    pe.wait_ge(h_ready, c + 1)
                    for tt in range(TT):
                        cols = slice(tt * P, (tt + 1) * P)
                        wc = slice((c % 2) * CW, (c % 2 + 1) * CW)
                        last = three(psum[tt][:], hh[:, c, cols], hl[:, c, cols], wh[:, U_V + j, wc], wl[:, U_V + j, wc],
                                     c == 0, c == DC - 1)
                        if c == 2 * j + 1 and tt == TT - 1:
                            last.then_inc(unit_used, 1)
                        last = three(psum[4][:, tt * HEADS:(tt + 1) * HEADS], hh[:, c, cols], hl[:, c, cols],
                                     wf_h[:, c, :], wf_l[:, c, :], c == 0 and tt == 0, c == DC - 1 and tt == TT - 1)
            last.then_inc(f_ready, 1)

            pe.wait_ge(v_out, 1)
            project(U_MIX, 0)
            project(U_MIX + 1, 1)
            pe.wait_ge(logf_ready, 1)
            for j in range(TT):
                last = nc.tensor.matmul(psum[5][0:HEADS, j * P:T], logf[:, j, :], tri[:, 0:T - j * P],
                                        start=j == 0, stop=j == TT - 1)
            last.then_inc(cum_ready, 1)

            def rows(e):
                return slice(0, HD + 2) if e == 0 else slice(0, P)

            def transposes(g):
                e, qi = (g // TT) % 2, g % TT
                pe.wait_ge(probs_ready, g + 1)
                if g >= 1:
                    pe.wait_ge(pT_out, g)
                for kj in range(qi + 1):
                    last = nc.tensor.transpose(psum[5][:, kj * P:(kj + 1) * P], probs[g % 3][:, kj * P:(kj + 1) * P], ident[:])
                last.then_inc(pT_ready, 1)

            def values(g):
                pair, e, qi = g // (2 * TT), (g // TT) % 2, g % TT
                pe.wait_ge(pT_out, g + 1)
                if g % (2 * TT) == 0 and pair >= 2:
                    pe.wait_ge(pair_out, pair - 1)
                head = 2 * pair + e
                for kj in range(qi + 1):
                    last = nc.tensor.matmul(psum[6 + pair % 2][HD * e:HD * (e + 1), qi * P:(qi + 1) * P],
                                            v_sb[:, kj, head * HD:(head + 1) * HD], probsT[:, kj * P:(kj + 1) * P],
                                            start=kj == 0, stop=kj == qi)
                last.then_inc(pv_done, 1)

            for pair in range(PAIRS):
                for s in range(2 * TT):
                    for k in pair_share(pair, s):
                        mu, c = 2 + k // DC, k % DC
                        if c == 0 and mu >= 3:
                            wait_mix_out(pe, mu - 3)
                        last = project(U_MIX + mu, mu % 3, c, c + 1)
                    g = 2 * TT * pair + s
                    e, qi = s // TT, s % TT
                    if s == 0:
                        pe.wait_ge(aug_in[pair % 2], 64 * (pair // 2 + 1))
                        wait_mix_out(pe, 5 * pair if pair else 1)
                    if g >= 2:
                        pe.wait_ge(exp_done, g - 1)
                    nc.tensor.matmul(psum[3 + g % 2][:, 0:(qi + 1) * P], qa[rows(e), pair % 2, e, qi * P:(qi + 1) * P],
                                     ka[rows(e), pair % 2, e, 0:(qi + 1) * P], start=True, stop=True).then_inc(logits_ready, 1)
                    if g >= 2:
                        transposes(g - 2)
                    if g >= 3:
                        values(g - 3)
            last_g = 2 * TT * PAIRS - 1
            transposes(last_g - 1)
            values(last_g - 2)
            for k in (3, 2, 1):
                wait_mix_out(pe, len(MIX) - k)
            project(U_MERGE, 0)
            transposes(last_g)
            values(last_g - 1)
            project(U_MERGE + 1, 1)
            values(last_g)

            for dc in range(DC):
                n, b = U_MERGE + 3 * dc, 4 * (dc % 2)
                if dc >= 2:
                    pe.wait_ge(mg_out, dc - 1)
                if dc >= 1:
                    project(n, b)
                    project(n + 1, b + 1)
                pe.wait_ge(lo_done, n + 3)
                if dc == 0:
                    pe.wait_ge(exp_done, 2 * TT * PAIRS)
                for br, bh, bl in ((1, conv_h, conv_l), (0, attn_h, attn_l)):
                    if dc == 0 and br == 0:
                        pe.wait_ge(pair_out, PAIRS)
                    for c in range(CC):
                        last = three(psum[b + 2 + br][:], w(wh, n + 2, br * CC + c), w(wl, n + 2, br * CC + c),
                                     bh[:, c, :], bl[:, c, :], c == 0, c == CC - 1)
                last.then_inc(unit_used, 1)

            pe.wait_ge(mg_out, DC)
            project_pair(U_OUT, 0, ml_ready, 0)
            for dc in range(2, DC):
                if dc >= 4:
                    pe.wait_ge(wo_out, dc - 3)
                project(U_OUT + dc, dc % 4)

            norm_sums(1)

            def score(n):
                pe.wait_ge(pq_out, n + 1)
                if n == 0:
                    pe.wait_ge(keys_in, 16)
                if n >= 2:
                    pe.wait_ge(sc_out, n - 1)
                for tt in range(TT):
                    last = nc.tensor.matmul(psum[2 + n % 2][:, tt * NK:(tt + 1) * NK], qT[:, n % 2, tt * P:(tt + 1) * P],
                                            keys[:, n, :], start=True, stop=True)
                last.then_inc(sc_ready, 1)

            pe.wait_ge(wo_out, DC)
            project_pair(U_PQ, 0, h_ready, DC)
            score(0)
            for n in range(2, N_PQ):
                pe.wait_ge(pq_out, n - 1)
                project(U_PQ + n, n % 2)
                score(n - 1)
            score(N_PQ - 1)

            def block_scores(slot, lo_needed, bank, c0=0, c1=DC):
                for c in range(c0, c1):
                    if c == 0:
                        pe.wait_ge(lo_done, lo_needed)
                    cols = slice(c * P, (c + 1) * P)
                    last = three(psum[bank][:], wh[:, slot, cols], wl[:, slot, cols], hh[:, c, :], hl[:, c, :],
                                 c == 0, c == DC - 1)
                if c1 == DC:
                    last.then_inc(unit_used, 1)

            def chosen_transposed(tt):
                for k in range(3):
                    pe.wait_ge(chosen_ready, 3 * tt + k + 1)
                    nc.tensor.transpose(psum[4 + k][:, tt * P:(tt + 1) * P], chosen[:, tt % 2, k, :], ident[:]).then_inc(chT_ready, 1)

            pe.wait_ge(sc_out, N_PQ)
            for u in range(ROUTE_U):
                for tt in range(TT):
                    if CHOSEN_AT[tt] == u:
                        chosen_transposed(tt)
                if u < 2:
                    pe.wait_ge(pq_out, N_PQ)
                else:
                    pe.wait_ge(early_done, u - 1)
                block_scores(u % SL, U_DENSE + u + 1, u % 2)
            for tt in range(TT):
                if CHOSEN_AT[tt] == ROUTE_U:
                    chosen_transposed(tt)

            quads, share = P // QUAD, GATE_U * DC * QUAD // P

            def gates_of(i, first):
                for q in range(quads):
                    if not (first and q < 4):
                        pe.wait_ge(quad_out, quads * i + (q - 3))
                    batch = q * QUAD // HB
                    pe.wait_ge(hot_ready, P // HB * i + (batch + 1))
                    u, c0 = q * share // DC, q * share % DC
                    if c0 == 0:
                        pe.wait_ge(early_done, GATE_U * i + (ROUTE_U + u - 1))
                        pe.wait_ge(lo_done, U_GATE + GATE_U * i + (u + 1))
                    slot = (U_GATE + u) % SL
                    for n in range(3 * share):
                        c, which = c0 + n // 3, n % 3
                        cols = slice(c * P, (c + 1) * P)
                        last = nc.tensor.matmul(psum[u % 2][:], (wl if which == 2 else wh)[:, slot, cols],
                                                (hl if which == 1 else hh)[:, c, :],
                                                start=c == 0 and which == 0, stop=c == DC - 1 and which == 2)
                        if n < 2 * QUAD:
                            k, part = n // 2, n % 2
                            tok = q * QUAD % HB + k
                            small = nc.tensor.matmul(psum[2 + q % 4][:, k * NK:(k + 1) * NK], hot[:, batch % 2, 0, tok, :],
                                                     hot[:, batch % 2, 1 + part, tok, :], start=part == 0, stop=part == 1)
                            if n == 2 * QUAD - 1:
                                small.then_inc(quad_done, 1)
                    if c0 + share == DC:
                        last.then_inc(unit_used, 1)

            pe.wait_ge(chT_out, 3)
            gates_of(0, True)
            with pe.Fori(1, TT) as i:
                gates_of(i, False)

            def scores_of(first_slot, unit0, blocks_before):
                for j in range(GB):
                    if blocks_before is not None:
                        pe.wait_ge(w_done, blocks_before + (j + 1))
                    block_scores(first_slot + j, unit0 + (j + 1), j)

            def values_of(first_slot, unit0, parity, blocks, outs_before):
                pe.wait_ge(lo_done, unit0 + GB)
                pe.wait_ge(wsplit, blocks)
                for dc in range(DC):
                    if outs_before is not None or dc >= 4:
                        pe.wait_ge(o_out, (0 if outs_before is None else outs_before) + (dc - 3))
                    for j in range(GB):
                        last = three(psum[4 + dc % 4][:], wh[:, first_slot + j, dc * P:(dc + 1) * P],
                                     wl[:, first_slot + j, dc * P:(dc + 1) * P],
                                     act_h[:, parity, j, :], act_l[:, parity, j, :], j == 0, j == GB - 1)
                        if dc == DC - 1:
                            last.then_inc(unit_used, 1)
                    if dc < DC - 1:
                        last.then_inc(o_ready, 1)

            pe.wait_ge(quad_out, T // QUAD)
            pe.wait_ge(early_done, GB * EARLY)
            scores_of(U_S0 % SL, U_S0, None)
            values_of(U_V0 % SL, U_V0, 0, GB, None)
            values_of((U_V0 + GB) % SL, U_V0 + GB, 1, 2 * GB, DC)
            with pe.Fori(1, EARLY // 2) as i:
                for q in range(2):
                    values_of((U_V0 + GB * q) % SL, U_V0 + GB * q + 8 * i, q, GB * (1 + q) + 8 * i, DC * q + 16 * i)

            def turn_of(g, q, i):
                unit0 = U_SV + 2 * GB * (g + q - EARLY - 1)
                scores_of(U_SV % SL, unit0 + 16 * i, GB * (g + q - 1) + 8 * i)
                values_of((U_SV + GB) % SL, unit0 + GB + 16 * i, (g + q - 1) % 2, GB * (g + q) + 8 * i,
                          DC * (g + q - 1) + 16 * i)

            turn_of(EARLY + 1, 0, 0)
            with pe.Fori(0, (GROUPS - EARLY - 2) // 2) as i:
                for q in range(2):
                    turn_of(EARLY + 2, q, i)
            values_of((U_PLE - GB) % SL, U_PLE - GB, (GROUPS - 1) % 2, NK, DC * (GROUPS - 1))

            pe.wait_ge(w_done, NK)
            pe.wait_ge(pp_split, 4)
            for half in range(2):
                emb = U_PLE + 5 * half
                pe.wait_ge(lo_done, emb + 1)
                for k4 in range(4):
                    if half == 1:
                        pe.wait_ge(ple_out, k4 + 1)
                    elif k4 >= 2:
                        pe.wait_ge(o_out, DC * (GROUPS - 1) + k4 + 3)
                    for k in range(2):
                        last = three(psum[2 + k4][:], w(wh, emb, 2 * k4 + k), w(wl, emb, 2 * k4 + k),
                                     pt_h[:, k, :], pt_l[:, k, :], k == 0, k == 1)
                last.then_inc(unit_used, 1)
                if half == 0:
                    norm_sums(2)
                    project_pair(emb + 1, 0, h_ready, 2 * DC)
                for dc in range(2 if half == 0 else 4, 4 * half + 4):
                    pe.wait_ge(ple_out, dc - 1)
                    project(emb + 1 + dc % 4, dc % 2)
            norm_sums(3)

        @block.scalar
        def _(act):
            for dst, src in ((gain, gains), (wf, w_f), (bfb, b_f), (convw, conv_w)):
                act.dma_start(dst[:], src).then_inc(const_in, 16)

            def high(n, turn=None):
                act.wait_ge(raw_in[n % RAW], 16 * (n // RAW + 1) if turn is None else turn)
                nc.scalar.activation(wh[:, n % SL, :], raw[:, n % RAW, :], ACT.Copy).then_inc(hi_done, 1)

            def next_high(n, i=None):
                if i is None:
                    if n + SL < N_UNITS:
                        act.wait_ge(unit_used, n + 1)
                        high(n + SL)
                else:
                    step, i = i
                    act.wait_ge(unit_used, step * i + (n + 1))
                    high(n + SL, 16 * step // RAW * i + 16 * ((n + SL) // RAW + 1))

            def square(k, sqb, c):
                if c >= 2:
                    act.wait_ge(sq_used, DC * k + c - 1)
                nc.scalar.activation(sqb[:, c % 2, :], x[:, c, :], ACT.Square).then_inc(sq_ready, 1)

            def root(k):
                act.wait_ge(sum_ready, k + 1)
                nc.scalar.activation(factor[:], psum[6][:, 0:TT], ACT.Sqrt, bias=eps[:]).then_inc(std_ready, 1)

            def norm(k, hfb, highs=()):
                root(k)
                for c in range(DC):
                    act.wait_ge(hf_ready, DC * k + c + 1)
                    nc.scalar.activation(hh[:, c, :], hfb[:, c % 2, :], ACT.Copy).then_inc(hh_ready, 1)
                    for after, n in highs:
                        if after == c:
                            high(n)

            for c in range(DC):
                act.wait_ge(x_in[c // 2], 16)
                square(0, sq, c)
            high(0)
            norm(0, hf, highs=((0, 1), (2, 2), (4, 3), (6, 4)))
            for n in range(5, SL):
                high(n)
            for n in range(3):
                next_high(U_V + n)
            act.wait_ge(unit_used, U_V + 4)
            for tt in range(TT):
                last = nc.scalar.activation(v_sb[:, tt, :], psum[tt][:], ACT.Copy)
            last.then_inc(v_out, 1)
            next_high(U_V + 3)
            act.wait_ge(f_abs, 1)
            nc.scalar.activation(fe[:], fa[:], ACT.Exp, scale=-1.0).then_inc(f_exp, 1)
            act.wait_ge(f_exp, 1)
            nc.scalar.activation(fa[:], fe[:], ACT.Ln, bias=ones[:, 0:1]).then_inc(f_ln, 1)

            def gate_rows(pair):
                if pair == 0:
                    act.wait_ge(cum_out, 2)
                if pair >= 2:
                    act.wait_ge(logits_ready, 2 * TT * (pair - 1))
                for e, (rq, rk) in enumerate(((HD, HD + 1), (0, 1))):
                    h = 2 * pair + e
                    act.dma_start(qa[rq:rq + 1, pair % 2, e, :], cum[h:h + 1, :]).then_inc(aug_in[pair % 2], 16)
                    act.dma_start(ka[rk:rk + 1, pair % 2, e, :], ncum[h:h + 1, :]).then_inc(aug_in[pair % 2], 16)

            def mix_out(m):
                act.wait_ge(unit_used, U_MIX + m + 1)
                kind = MIX[m]
                pair = (m + 3) // 5 if kind in "qk" else (m - 2) // 5
                if kind == "C":
                    if pair >= 1:
                        act.wait_ge(mix_dve, 2 * pair - 1)
                    nc.scalar.activation(c_in, psum[m % 3][:], ACT.Copy).then_inc(mix_act, 1)
                    return
                dst = qa if kind == "q" else ka
                scale = HD ** -0.5 if kind == "q" else 1.0
                if m == 0:
                    act.wait_ge(rows_ready, 1)
                if pair >= 2:
                    act.wait_ge(logits_ready, 2 * TT * (pair - 1))
                for e in range(2):
                    r = slice(HD * e, HD * (e + 1))
                    last = nc.scalar.activation(dst[r, pair % 2, e, :], psum[m % 3][r, :], ACT.Copy, scale=scale)
                last.then_inc(mix_act, 1)

            mix_out(0)
            next_high(U_MIX)
            mix_out(1)
            next_high(U_MIX + 1)
            gate_rows(0)
            gate_rows(1)

            def probs_out(g):
                act.wait_ge(pT_ready, g + 1)
                if g >= 1:
                    act.wait_ge(pv_done, g)
                qi = g % TT
                nc.scalar.activation(probsT[:, 0:(qi + 1) * P], psum[5][:, 0:(qi + 1) * P], ACT.Copy).then_inc(pT_out, 1)

            for pair in range(PAIRS):
                for s in range(2 * TT):
                    for k in pair_share(pair, s):
                        mu = 2 + k // DC
                        if k % DC == DC - 1 and MIX[mu] in "qkC":
                            if MIX[mu] == "q" and mu > 4:
                                gate_rows((mu + 3) // 5)
                            mix_out(mu)
                        if k % DC == DC - 1:
                            next_high(U_MIX + mu)
                    g = 2 * TT * pair + s
                    qi = s % TT
                    act.wait_ge(max_ready, g + 1)
                    if g >= 3:
                        act.wait_ge(pT_ready, g - 2)
                    nc.scalar.activation(probs[g % 3][:, 0:(qi + 1) * P], psum[3 + g % 2][:, 0:(qi + 1) * P], ACT.Exp,
                                         bias=nmax[:, g % 3:g % 3 + 1],
                                         accum_out=rsum[:, g % 3:g % 3 + 1]).then_inc(exp_done, 1)
                    if g >= 2:
                        probs_out(g - 2)
            probs_out(2 * TT * PAIRS - 2)
            probs_out(2 * TT * PAIRS - 1)

            for dc in range(DC):
                b = 4 * (dc % 2)
                for k, buf in enumerate((sig_a, sig_c)):
                    act.wait_ge(unit_used, U_MERGE + 3 * dc + k + 1)
                    if dc >= 2:
                        act.wait_ge(mg_out, dc - 1)
                    elif dc == 0:
                        act.wait_ge(pv_done, 2 * TT * PAIRS)
                        act.wait_ge(mix_dve, by_dve(len(MIX)))
                    nc.scalar.activation(buf[:, dc % 2, :], psum[b + k][:], ACT.Sigmoid).then_inc(sig_done, 1)
                    next_high(U_MERGE + 3 * dc + k)
                next_high(U_MERGE + 3 * dc + 2)
            for c in range(DC):
                if c == 0:
                    act.wait_ge(unit_used, U_OUT)
                act.wait_ge(mg_out, c + 1)
                nc.scalar.activation(hh[:, c, :], merged[:, c, :], ACT.Copy).then_inc(mh_ready, 1)

            act.dma_start(keys[:], keysT).then_inc(keys_in, 16)
            for c in range(DC):
                act.wait_ge(wo_out, c + 1)
                square(1, sq1, c)
                next_high(U_OUT + c)
            norm(1, hf1)

            def score_out(n):
                act.wait_ge(sc_ready, n + 1)
                if n >= 2:
                    act.wait_ge(sc_used, n - 1)
                nc.scalar.activation(scores[:, n % 2], psum[2 + n % 2][:].rearrange("p (t n) -> p t n", t=TT),
                                     ACT.Copy).then_inc(sc_out, 1)

            for n in range(N_PQ):
                act.wait_ge(unit_used, U_PQ + n + 1)
                if n >= 2:
                    act.wait_ge(sc_ready, n - 1)
                nc.scalar.activation(qT[:, n % 2, :], psum[n % 2][:], ACT.Copy).then_inc(pq_out, 1)
                next_high(U_PQ + n)
                if n >= 1:
                    score_out(n - 1)
            score_out(N_PQ - 1)

            def early_gelu(bank, buf, used, before):
                act.wait_ge(unit_used, used)
                if before is not None:
                    act.wait_ge(gelu_out[buf], before)
                nc.scalar.activation(gout[:, buf, :], psum[bank][:], ACT.Gelu).then_inc(early_done, 1)

            def store_gelu(buf, done, block):
                act.wait_ge(early_done, done)
                act.dma_start(gelu_dram[block], gout[:, buf, :]).then_inc(gelu_out[buf], 16)

            for u in range(ROUTE_U):
                for tt in range(TT):
                    if EXP_AT[tt] == u:
                        act.wait_ge(top_ready, tt + 1)
                        nc.scalar.activation(top[:], top[:], ACT.Exp).then_inc(gexp, 1)
                early_gelu(u % 2, u % 4, U_DENSE + u + 1, 16 * (u // 4) if u >= 4 else None)
                next_high(U_DENSE + u)
                store_gelu(u % 4, u + 1, u)

            quads = P // QUAD

            def gates_of(i, first):
                for q in range(quads):
                    chunk, k = divmod(q, GT // QUAD)
                    act.wait_ge(quad_done, quads * i + (q + 1))
                    if k == 0 and not (first and chunk < 2):
                        act.wait_ge(stage_out[chunk % 2], 32 * i + 16 * (chunk // 2))
                    nc.scalar.activation(stage[:, chunk % 2, :, QUAD * k:QUAD * (k + 1)].rearrange("p a t -> p t a"),
                                         psum[2 + q % 4][:].rearrange("p (t a) -> p t a", t=QUAD), ACT.Copy).then_inc(quad_out, 1)
                    if q % (quads // GATE_U) == quads // GATE_U - 1:
                        u = q // (quads // GATE_U)
                        early_gelu(u % 2, u % 4, U_GATE + GATE_U * i + (u + 1),
                                   16 * (ROUTE_U // 4) + 16 * (GATE_U // 4) * i + 16 * (u // 4))
                        if first:
                            next_high(U_GATE + u)
                        else:
                            next_high(U_GATE + u, (GATE_U, i))
                        store_gelu(u % 4, GATE_U * i + (ROUTE_U + u + 1),
                                   ROUTE_U + u if first else bass.ds(GATE_U * i + (ROUTE_U + u), 1))
                    if k == GT // QUAD - 1:
                        act.wait_ge(quad_out, quads * i + (q + 1))
                        dst = gate_dram[chunk] if first else gate_dram[bass.ds((P // GT) * i + chunk, 1)].rearrange("o b a t -> (o b) a t")
                        act.dma_start(dst, stage[:, chunk % 2]).then_inc(stage_out[chunk % 2], 16)

            gates_of(0, True)
            with act.Fori(1, TT) as i:
                gates_of(i, False)
            for par in range(2):
                act.wait_ge(stage_out[par], 16 * (CH // 2))
            for buf in range(4):
                act.wait_ge(gelu_out[buf], 16 * (GB * EARLY // 4))

            def load_gates(parity, blocks):
                act.dma_start(gate[:, parity], gate_dram[:, :, blocks, :].rearrange("c b a t -> b c a t")).then_inc(gate_in[parity], 16)

            def load_gelus(parity, blocks):
                act.dma_start(gelu_in[:, parity], gelu_dram[blocks].rearrange("a b t -> b a t")).then_inc(gelu_back[parity], 16)

            def gelus(unit0, i=None):
                for j in range(GB):
                    act.wait_ge(unit_used, unit0 + (j + 1) if i is None else 16 * i + (unit0 + (j + 1)))
                    nc.scalar.activation(psum[j][:], psum[j][:], ACT.Gelu).then_inc(gelu_done, 1)
                    next_high(unit0 + j, None if i is None else (16, i))

            def highs_after(unit0, i=None):
                for j in range(GB):
                    next_high(unit0 + j, None if i is None else (16, i))

            for g in range(2):
                load_gates(g, slice(GB * g, GB * g + GB))
                load_gelus(g, slice(GB * g, GB * g + GB))
            gelus(U_S0)
            with act.Fori(0, (EARLY - 2) // 2) as i:
                for q in range(2):
                    act.wait_ge(w_done, GB * (1 + q) + 8 * i)
                    load_gates(q, bass.ds(GB * (2 + q) + 8 * i, GB))
                    load_gelus(q, bass.ds(GB * (2 + q) + 8 * i, GB))
                    for j in range(GB):
                        next_high(U_V0 + GB * q + j, (8, i))
            for q in range(2):
                g = EARLY - 2 + q
                act.wait_ge(w_done, GB * (g + 1))
                load_gates(q, slice(GB * (g + 2), GB * (g + 3)))
                highs_after(U_V0 + GB * g)

            def turn_of(g, q, i):
                unit0 = U_SV + 2 * GB * (g + q - EARLY - 1)
                gelus(unit0, i)
                if i is None:
                    act.wait_ge(w_done, GB * g)
                    load_gates((g + 1) % 2, slice(GB * (g + 1), GB * (g + 2)))
                else:
                    act.wait_ge(w_done, GB * (g + q) + 8 * i)
                    load_gates((g + q + 1) % 2, bass.ds(GB * (g + q + 1) + 8 * i, GB))
                highs_after(unit0 + GB, i)

            turn_of(EARLY + 1, 0, None)
            with act.Fori(0, (GROUPS - EARLY - 2) // 2 - 1) as i:
                for q in range(2):
                    turn_of(EARLY + 2, q, i)
            for g in (GROUPS - 2, GROUPS - 1):
                unit0 = U_SV + 2 * GB * (g - EARLY - 1)
                gelus(unit0)
                if g == GROUPS - 2:
                    act.wait_ge(w_done, GB * g)
                    load_gates((g + 1) % 2, slice(GB * (g + 1), GB * (g + 2)))
                highs_after(unit0 + GB)
            act.wait_ge(w_done, NK)
            act.dma_start(pt[:], pT).then_inc(p_in, 16)
            for c in range(DC):
                act.wait_ge(o_out, DC * (GROUPS - 1) + c + 1)
                square(2, sq2, c)
            highs_after(U_PLE - GB)
            norm(2, hf2)
            next_high(U_PLE)
            next_high(U_PLE + 1)
            for dc in range(DC):
                act.wait_ge(unit_used, U_PLE + 5 * (dc // 4) + dc % 4 + 2)
                if dc >= 2:
                    act.wait_ge(ple_out, dc - 1)
                nc.scalar.activation(sg[:, dc % 2, :], psum[dc % 2][:], ACT.Sigmoid).then_inc(ple_sig, 1)
                if dc >= 1:
                    act.wait_ge(ple_out, dc)
                    square(3, sq2, dc - 1)
            act.wait_ge(ple_out, DC)
            square(3, sq2, DC - 1)
            root(3)

        @block.vector
        def _(dve):
            chain = [0]

            def mark(ins):
                chain[0] += 1
                ins.then_inc(dve_own, 1)

            def link(ins):
                mark(ins)
                dve.wait_ge(dve_own, chain[0])

            def add_square(k, sqb, c):
                dve.wait_ge(sq_ready, DC * k + c + 1)
                if c == 0:
                    nc.vector.tensor_copy(rstd[:], sqb[:, 0, :]).then_inc(sq_used, 1)
                else:
                    dve.wait_ge(sq_used, DC * k + c)
                    nc.vector.tensor_tensor(rstd[:], rstd[:], sqb[:, c % 2, :], ALU.add).then_inc(sq_used, 1)

            def norm(k, hfb):
                dve.wait_ge(std_ready, k + 1)
                link(nc.vector.reciprocal(factor[:], factor[:]))
                for tt in range(TT):
                    nc.vector.tensor_scalar(rstd[:, tt * P:(tt + 1) * P], ident[:], factor[:, tt:tt + 1], None,
                                            ALU.mult).then_inc(diag_ready, 1)
                dve.wait_ge(row_ready, k + 1)
                if k == 3:
                    for c in range(DC):
                        nc.vector.scalar_tensor_tensor(out=outb[:, c, :], in0=x[:, c, :], scalar=gain[:, k, c:c + 1],
                                                       in1=psum[7][:], op0=ALU.mult, op1=ALU.mult).then_inc(out_ready, 1)
                    return
                for c in range(DC + 1):
                    if c < DC:
                        if c >= 2:
                            dve.wait_ge(h_ready, DC * k + c - 1)
                        nc.vector.scalar_tensor_tensor(out=hfb[:, c % 2, :], in0=x[:, c, :], scalar=gain[:, k, c:c + 1],
                                                       in1=psum[7][:], op0=ALU.mult, op1=ALU.mult).then_inc(hf_ready, 1)
                    if c >= 1:
                        dve.wait_ge(hf_ready, DC * k + c)
                        dve.wait_ge(hh_ready, DC * k + c)
                        nc.vector.tensor_tensor(hl[:, c - 1, :], hfb[:, (c - 1) % 2, :], hh[:, c - 1, :].bitcast(F32),
                                                ALU.subtract).then_inc(h_ready, 1)

            for c in range(DC):
                if c == 4:
                    dve.wait_ge(const_in, 64)
                    link(nc.vector.tensor_copy(wf_h[:], wf[:]))
                    nc.vector.tensor_tensor(wf_l[:], wf[:], wf_h[:].bitcast(F32), ALU.subtract).then_inc(wf_split, 1)
                add_square(0, sq, c)
            norm(0, hf)
            link(nc.vector.memset(qa[0:HD, :, 1, :], 0.0))
            link(nc.vector.memset(ka[0:HD, :, 1, :], 0.0))
            nc.vector.memset(qa[0:2, :, 1, :], 1.0)
            nc.vector.memset(ka[0:2, :, 1, :], 1.0)
            nc.vector.memset(qa[HD:HD + 2, :, 0, :], 1.0)
            nc.vector.memset(z[:, 0:TAPS - 1], 0.0)
            link(nc.vector.memset(ka[HD:HD + 2, :, 0, :], 1.0))
            nc.vector.memset(nmax[:], 0.0).then_inc(rows_ready, 1)

            dve.wait_ge(f_ready, 1)
            link(nc.vector.tensor_tensor(fz[:], psum[4][:, 0:TT * HEADS].rearrange("p (t h) -> p t h", t=TT),
                                         bfb[:].unsqueeze(1).to_broadcast([P, TT, HEADS]), ALU.add))
            link(nc.vector.tensor_scalar(fe[:], fz[:], -1.0, None, ALU.mult))
            nc.vector.tensor_tensor(fa[:], fz[:], fe[:], ALU.max).then_inc(f_abs, 1)
            link(nc.vector.tensor_scalar(fz[:], fz[:], 0.0, None, ALU.min))
            dve.wait_ge(f_ln, 1)
            nc.vector.tensor_tensor(logf[:], fz[:], fa[:], ALU.subtract).then_inc(logf_ready, 1)
            dve.wait_ge(cum_ready, 1)
            nc.vector.tensor_copy(cum[:], psum[5][0:HEADS, :]).then_inc(cum_out, 1)
            nc.vector.tensor_scalar(ncum[:], psum[5][0:HEADS, :], -1.0, None, ALU.mult).then_inc(cum_out, 1)

            def mix_out(m):
                kind, pair = MIX[m], (m - 2) // 5
                dve.wait_ge(unit_used, U_MIX + m + 1)
                if kind == "x":
                    dve.wait_ge(mix_act, by_act(m))
                    nc.vector.tensor_tensor(z[:, TAPS - 1:], psum[m % 3][:], c_in, ALU.mult).then_inc(mix_dve, 1)
                    dve.wait_ge(mix_dve, by_dve(m) + 1)
                    link(nc.vector.tensor_scalar(cv, z[:, 2:2 + T], convw[:, 2, pair:pair + 1], None, ALU.mult))
                    for tap in (1, 0):
                        link(nc.vector.scalar_tensor_tensor(out=cv, in0=z[:, tap:tap + T], scalar=convw[:, tap, pair:pair + 1],
                                                            in1=cv, op0=ALU.mult, op1=ALU.add))
                    return
                nc.vector.tensor_tensor(cv, psum[m % 3][:], cv, ALU.mult).then_inc(mix_dve, 1)
                dve.wait_ge(mix_dve, by_dve(m) + 1)
                link(nc.vector.tensor_copy(conv_h[:, pair, :], cv))
                link(nc.vector.tensor_tensor(conv_l[:, pair, :], cv, conv_h[:, pair, :].bitcast(F32), ALU.subtract))

            def pair_done(pair):
                dve.wait_ge(pv_done, 2 * TT * (pair + 1))
                bank = psum[6 + pair % 2]
                link(nc.vector.tensor_copy(attn_h[:, pair, :], bank[:]))
                nc.vector.tensor_tensor(attn_l[:, pair, :], bank[:], attn_h[:, pair, :].bitcast(F32),
                                        ALU.subtract).then_inc(pair_out, 1)

            for pair in range(PAIRS):
                for s in range(2 * TT):
                    for k in pair_share(pair, s):
                        mu = 2 + k // DC
                        if k % DC == DC - 1 and MIX[mu] in "xB":
                            mix_out(mu)
                    g = 2 * TT * pair + s
                    qi = s % TT
                    bank = psum[3 + g % 2]
                    diag = bank[:, qi * P:(qi + 1) * P]
                    dve.wait_ge(logits_ready, g + 1)
                    link(nc.vector.tensor_tensor(diag, diag, mask[:], ALU.add))
                    nc.vector.tensor_reduce(nmax[:, g % 3:g % 3 + 1], bank[:, 0:(qi + 1) * P], AX.X, ALU.max,
                                            negate=True).then_inc(max_ready, 1)
                    dve.wait_ge(exp_done, g + 1)
                    link(nc.vector.reciprocal(rsum[:, g % 3:g % 3 + 1], rsum[:, g % 3:g % 3 + 1]))
                    row = probs[g % 3][:, 0:(qi + 1) * P]
                    nc.vector.tensor_scalar(row, row, rsum[:, g % 3:g % 3 + 1], None, ALU.mult).then_inc(probs_ready, 1)
                    if pair >= 1 and s == 3:
                        pair_done(pair - 1)
            pair_done(PAIRS - 1)

            for dc in range(DC):
                b = 4 * (dc % 2)
                dve.wait_ge(unit_used, U_MERGE + 3 * dc + 3)
                dve.wait_ge(sig_done, 2 * dc + 2)
                mark(nc.vector.tensor_tensor(sig_a[:, dc % 2, :], psum[b + 2][:], sig_a[:, dc % 2, :], ALU.mult))
                link(nc.vector.tensor_tensor(sig_c[:, dc % 2, :], psum[b + 3][:], sig_c[:, dc % 2, :], ALU.mult))
                nc.vector.tensor_tensor(merged[:, dc, :], sig_a[:, dc % 2, :], sig_c[:, dc % 2, :], ALU.add).then_inc(mg_out, 1)
            for c in range(DC):
                dve.wait_ge(mg_out, c + 1)
                dve.wait_ge(mh_ready, c + 1)
                nc.vector.tensor_tensor(hl[:, c, :], merged[:, c, :], hh[:, c, :].bitcast(F32), ALU.subtract).then_inc(ml_ready, 1)
            for dc in range(DC):
                dve.wait_ge(unit_used, U_OUT + dc + 1)
                nc.vector.tensor_tensor(x[:, dc, :], psum[dc % 4][:], x[:, dc, :], ALU.add).then_inc(wo_out, 1)
                if dc >= 1:
                    add_square(1, sq1, dc - 1)
            add_square(1, sq1, DC - 1)
            norm(1, hf1)

            def best(rows):
                own = [0] * len(rows)
                for step in range(5):
                    for k, (values, vals, idx) in enumerate(rows):
                        if step:
                            dve.wait_ge(dve_own, own[k])
                        half = slice(0, 8) if step < 3 else slice(8, 16)
                        if step in (0, 3):
                            mark(nc.vector.max(vals[:, half], values))
                        elif step in (1, 4):
                            mark(nc.vector.max_index(idx[:, half], vals[:, half], values))
                        else:
                            mark(nc.vector.match_replace(values, vals[:, half], values, MASKED))
                        own[k] = chain[0]

            for n in range(N_PQ):
                dve.wait_ge(sc_out, n + 1)
                best([(scores[:, n % 2, tt, :], v12[:, tt, n, :], i12[:, tt, n, :]) for tt in range(TT)])
                dve.wait_ge(dve_own, chain[0])
                nc.vector.memset(gsum[:, 0, 0:1], 0.0).then_inc(sc_used, 1)

            for tt in range(TT):
                vv = v12[:, tt].rearrange("p (h s) k -> p h s k", s=2)
                link(nc.vector.tensor_tensor(cand[:], vv[:, :, 0, :].unsqueeze(3).to_broadcast([P, PH, TOPK, TOPK]),
                                             vv[:, :, 1, :].unsqueeze(2).to_broadcast([P, PH, TOPK, TOPK]), ALU.add))
                best([(cand[:, h, :, :].rearrange("p a b -> p (a b)"), top[:, h, :], topj[:, h, :]) for h in range(PH)])
                dve.wait_ge(dve_own, chain[0])
                link(nc.vector.tensor_copy(gsum[:, 1, :], top[:, :, 0]))
                nc.vector.tensor_tensor(top[:], top[:], gsum[:, 1, :].unsqueeze(2).to_broadcast([P, PH, TOPK]),
                                        ALU.subtract).then_inc(top_ready, 1)
                tj = topj[:].rearrange("p h k -> p (h k)")
                mark(nc.vector.tensor_scalar(rank[:, 0, :], tj, 4, None, ALU.logical_shift_right))
                mark(nc.vector.tensor_scalar(rank[:, 1, :], tj, TOPK - 1, None, ALU.bitwise_and))
                mark(nc.vector.tensor_copy(i12b[:], i12[:, tt]))
                dve.wait_ge(dve_own, chain[0] - 1)
                link(nc.vector.tensor_copy(rankb[:], rank[:]))
                ii = i12b[:].rearrange("p (h s) k -> p h s k", s=2)
                for side in range(2):
                    if side == 0 and tt >= 2:
                        dve.wait_ge(chT_ready, 3 * (tt - 1))
                    elif side == 1:
                        dve.wait_ge(chosen_ready, 3 * tt + 1)
                    link(nc.vector.tensor_tensor(onehot[:], rankb[:, side, :].unsqueeze(2).to_broadcast([P, HK, TOPK]),
                                                 iota_k[:].unsqueeze(1).to_broadcast([P, HK, TOPK]), ALU.is_equal))
                    hot4 = onehot[:].rearrange("p (h k) r -> p h k r", h=PH)
                    link(nc.vector.tensor_tensor(hot4, hot4, ii[:, :, side, :].unsqueeze(2).to_broadcast([P, PH, TOPK, TOPK]),
                                                 ALU.mult))
                    nc.vector.tensor_reduce(chosen[:, tt % 2, side, :], onehot[:], AX.X, ALU.add).then_inc(chosen_ready, 1)
                dve.wait_ge(gexp, tt + 1)
                link(nc.vector.tensor_reduce(gsum[:, 0, :], top[:], AX.X, ALU.add))
                link(nc.vector.reciprocal(gsum[:, 0, :], gsum[:, 0, :]))
                nc.vector.tensor_tensor(chosen[:, tt % 2, 2, :].rearrange("p (h k) -> p h k", h=PH), top[:],
                                        gsum[:, 0, :].unsqueeze(2).to_broadcast([P, PH, TOPK]),
                                        ALU.mult).then_inc(chosen_ready, 1)
            dve.wait_ge(chT_ready, 3 * TT)
            nc.vector.tensor_copy(i1T[:], psum[4][:]).then_inc(chT_out, 1)
            nc.vector.tensor_copy(i2T[:], psum[5][:]).then_inc(chT_out, 1)
            nc.vector.tensor_copy(gT[:], psum[6][:]).then_inc(chT_out, 1)
            dve.wait_ge(chT_out, 3)
            link(nc.vector.tensor_copy(gT_h[:], gT[:]))
            link(nc.vector.tensor_tensor(gT_l[:], gT[:], gT_h[:].bitcast(F32), ALU.subtract))

            def one_hots(buf, batch, first):
                if not first:
                    dve.wait_ge(quad_done, HB // QUAD * batch - HB // QUAD)
                at = slice(HB * batch, HB * batch + HB) if first else bass.ds(HB * batch, HB)
                keys_b = iota_nk[:].unsqueeze(1).to_broadcast([P, HB, NK])
                first_key = hot[:, buf, 2].bitcast(F32)
                nc.vector.tensor_tensor(hot[:, buf, 2], keys_b, i1T[:, at].unsqueeze(2).to_broadcast([P, HB, NK]),
                                        ALU.is_equal).then_inc(hot_own, 1)
                nc.vector.tensor_tensor(hot[:, buf, 0], keys_b, i2T[:, at].unsqueeze(2).to_broadcast([P, HB, NK]), ALU.is_equal)
                dve.wait_ge(hot_own, 2 * batch + 1)
                nc.vector.tensor_tensor(hot[:, buf, 1], first_key,
                                        gT_h[:, at].bitcast(F32).unsqueeze(2).to_broadcast([P, HB, NK]), ALU.mult).then_inc(hot_own, 1)
                dve.wait_ge(hot_own, 2 * batch + 2)
                nc.vector.tensor_tensor(hot[:, buf, 2], first_key,
                                        gT_l[:, at].bitcast(F32).unsqueeze(2).to_broadcast([P, HB, NK]), ALU.mult).then_inc(hot_ready, 1)

            for k in range(2):
                one_hots(k, k, True)
            with dve.Fori(1, T // HB // 2) as i:
                for k in range(2):
                    one_hots(k, 2 * i + k, False)

            def weigh(parity, blocks, gate_turn, early_turn, buffer_free):
                for j in range(GB):
                    if early_turn is None:
                        dve.wait_ge(gelu_done, blocks + (j + 1 - GB * EARLY))
                        gelu = psum[j][:]
                    else:
                        gelu = gelu_in[:, parity, j, :]
                    if j == 0:
                        dve.wait_ge(gate_in[parity], gate_turn)
                        if early_turn is not None:
                            dve.wait_ge(gelu_back[parity], early_turn)
                        if buffer_free is not None:
                            dve.wait_ge(unit_used, buffer_free)
                    nc.vector.tensor_tensor(wt[:, j % 2, :].rearrange("p (c t) -> p c t", c=CH),
                                            gelu.rearrange("p (c t) -> p c t", c=CH), gate[:, parity, :, j, :],
                                            ALU.mult).then_inc(w_done, 1)
                    dve.wait_ge(w_done, blocks + (j + 1))
                    nc.vector.tensor_copy(act_h[:, parity, j, :], wt[:, j % 2, :]).then_inc(wcopy, 1)
                    dve.wait_ge(wcopy, blocks + (j + 1))
                    nc.vector.tensor_tensor(act_l[:, parity, j, :], wt[:, j % 2, :], act_h[:, parity, j, :].bitcast(F32),
                                            ALU.subtract).then_inc(wsplit, 1)

            def add_values(outs, unit0, squares=False):
                for dc in range(DC):
                    if dc < DC - 1:
                        dve.wait_ge(o_ready, outs + (dc + 1))
                    else:
                        dve.wait_ge(unit_used, unit0 + GB)
                    nc.vector.tensor_tensor(x[:, dc, :], psum[4 + dc % 4][:], x[:, dc, :], ALU.add).then_inc(o_out, 1)
                    if squares and dc >= 1:
                        add_square(2, sq2, dc - 1)

            SENT = DC - 1
            weigh(0, 0, 16, 16, None)
            weigh(1, GB, 16, 16, None)
            add_values(0, U_V0)
            with dve.Fori(0, (EARLY - 2) // 2) as i:
                for q in range(2):
                    g = 1 + q
                    weigh((g + 1) % 2, GB * (g + 1) + 8 * i, 16 * i + 32, 16 * i + 32, 8 * i + (U_V0 + GB * g))
                    add_values(SENT * g + 2 * SENT * i, U_V0 + GB * g + 8 * i)
            g = EARLY - 1
            weigh(0, GB * EARLY, 16 * (EARLY // 2 + 1), None, U_V0 + GB * g)
            add_values(SENT * g, U_V0 + GB * g)

            def turn_of(g, q, i):
                unit0 = U_SV + 2 * GB * (g + q - EARLY - 1)
                weigh((g + q) % 2, GB * (g + q) + 8 * i, 16 * ((g + q) // 2 + 1) + 16 * i, None, None)
                add_values(SENT * (g + q - 1) + 2 * SENT * i, unit0 + GB + 16 * i)

            turn_of(EARLY + 1, 0, 0)
            with dve.Fori(0, (GROUPS - EARLY - 2) // 2) as i:
                for q in range(2):
                    turn_of(EARLY + 2, q, i)
            dve.wait_ge(p_in, 16)
            for k in range(2):
                nc.vector.tensor_copy(pt_h[:, k, :], pt[:, k, :]).then_inc(pp_split, 1)
                dve.wait_ge(pp_split, 2 * k + 1)
                nc.vector.tensor_tensor(pt_l[:, k, :], pt[:, k, :], pt_h[:, k, :].bitcast(F32), ALU.subtract).then_inc(pp_split, 1)
            add_values(SENT * (GROUPS - 1), U_PLE - GB, squares=True)
            add_square(2, sq2, DC - 1)
            norm(2, hf2)
            for dc in range(DC):
                dve.wait_ge(ple_sig, dc + 1)
                link(nc.vector.tensor_tensor(upd[:, dc % 2, :], psum[2 + dc % 4][:], sg[:, dc % 2, :], ALU.mult))
                nc.vector.tensor_tensor(x[:, dc, :], x[:, dc, :], upd[:, dc % 2, :], ALU.add).then_inc(ple_out, 1)
                if dc >= 1:
                    add_square(3, sq2, dc - 1)
            add_square(3, sq2, DC - 1)
            norm(3, None)


def weight_stream(np, w_in, w_branch, w_out, w_peer_q, peer_u, peer_v, w_ple_gate, w_ple_proj):
    def tiles(w):
        k, n = w.shape
        return w.reshape(k // P, P, n // P, P).transpose(2, 1, 0, 3).reshape(n // P, P, -1)

    q, k, v, _, B, C, xc, ga, gc = np.split(w_in, np.cumsum([CW, CW, CW, HEADS, CW, CW, CW, D]), axis=1)
    vt = v.reshape(4, 2, P, CW).transpose(0, 2, 1, 3).reshape(4, P, UW)
    parts = {n: tiles(a) for n, a in (("q", q), ("k", k), ("C", C), ("x", xc), ("B", B))}
    at = dict.fromkeys(parts, 0)
    units = list(vt)
    for kind in MIX:
        units.append(parts[kind][at[kind]])
        at[kind] += 1
    ga, gc = tiles(ga), tiles(gc)
    branches = np.concatenate([tiles(w_branch[0]), tiles(w_branch[1])], axis=2)
    for dc in range(DC):
        units += [ga[dc], gc[dc], branches[dc]]
    units += list(tiles(w_out))
    units += list(tiles(w_peer_q.reshape(D, N_PQ * P)))
    u = peer_u.reshape(NK, NK, DC, P).transpose(0, 3, 2, 1).reshape(NK, P, UW)
    v = peer_v.reshape(NK, NK, D)
    group = [slice(GB * g, GB * g + GB) for g in range(GROUPS)]
    units += list(u[:GB * (EARLY + 1)])
    units += list(v[:GB * EARLY])
    for g in range(EARLY + 1, GROUPS):
        units += list(u[group[g]]) + list(v[group[g - 1]])
    units += list(v[group[-1]])
    gate = tiles(w_ple_gate)
    emb = w_ple_proj.reshape(2, P, 2, 4, P).transpose(2, 1, 3, 0, 4).reshape(2, P, UW)
    for half in range(2):
        units += [emb[half]] + list(gate[4 * half:4 * half + 4])
    return np.stack(units)


def kernel(**inputs):
    import numpy as np
    import concourse.bacc as bacc
    from concourse.bass_utils import run_bass_kernel_spmd

    a = {n: np.asarray(v) for n, v in inputs.items()}
    w_in = a["w_in"][0]
    arrays = {
        "xT": a["x"][0].T.reshape(DC, P, T),
        "pT": a["p"][0, 0].T.reshape(2, P, T).transpose(1, 0, 2),
        "stream": weight_stream(np, w_in, a["w_branch"][0], a["w_out"][0], a["w_peer_q"][0], a["peer_u"][0],
                                a["peer_v"][0], a["w_ple_gate"][0], a["w_ple_proj"][0]),
        "w_f": w_in[:, 3 * CW:3 * CW + HEADS].reshape(DC, P, HEADS).transpose(1, 0, 2),
        "b_f": np.broadcast_to(a["b_f"][0], (P, HEADS)),
        "conv_w": a["conv_w"][0].reshape(TAPS, CC, P).transpose(2, 0, 1),
        "gains": np.stack([a["g_mix"][0], a["g_ffn"][0], a["g_ple"][0], a["g_final"]]).reshape(4, DC, P).transpose(2, 0, 1),
        "keysT": np.stack([a["peer_k1"][0], a["peer_k2"][0]], axis=1).reshape(N_PQ, NK, P).transpose(2, 0, 1),
    }
    arrays = {n: np.ascontiguousarray(v) for n, v in arrays.items()}
    nc = bacc.Bacc("TRN2", target_bir_lowering=False, num_devices=1)
    args = {n: nc.dram_tensor(n, v.shape, mybir.dt.from_np(v.dtype), kind="ExternalInput").ap() for n, v in arrays.items()}
    gate_dram = nc.dram_tensor("gate_dram", (CH, P, NK, GT), F32, kind="Internal").ap()
    gelu_dram = nc.dram_tensor("gelu_dram", (GB * EARLY, P, T), F32, kind="Internal").ap()
    outT = nc.dram_tensor("outT", (DC, P, T), F32, kind="ExternalOutput").ap()
    peer_block_kernel(nc, gate_dram=gate_dram, gelu_dram=gelu_dram, outT=outT, **args)
    r = run_bass_kernel_spmd(nc, [arrays], core_ids=[0])
    return r.results[0]["outT"].reshape(D, T).T.reshape(1, T, D)
```
